# Optimizing a Trainium2 kernel written in Bass

```python
import math
import jax, jax.numpy as jnp
from jax import lax
import numpy as np

D_MODEL = 1024
BATCH = 1
SEQ = 256
DEPTH = 2

GRID_W = 64
NA_HEADS = 8
NA_HEAD_DIM = 64
NA_WIDTH = NA_HEADS * NA_HEAD_DIM
NA_KR_MAX = 8
NA_KW = 16
HY_WIDTH = 512
HY_SHORT = 3
HY_POS_BANDS = 16
HY_POS_DIM = 1 + 2 * HY_POS_BANDS
HY_FFN_HIDDEN = 64
HY_DECAY_TARGET = 1e-2
HY_FAST_PCT = 0.3
HY_SLOW_PCT = 1.5
HY_FILTER_SCALE = 0.03
N_BRANCHES = 2
IN_WIDTH = 3 * NA_WIDTH + 3 * HY_WIDTH + N_BRANCHES * D_MODEL
PEER_HEADS = 8
PEER_NKEYS = 128
PEER_N = PEER_NKEYS * PEER_NKEYS
PEER_DKEY = 256
PEER_TOPK = 16
PEER_CHUNK = 128
EPS = 1e-6

kernel_name = "hybrid_na_hyena_peer_encoder"

def rmsnorm(x, g):
    xf = x.astype(jnp.float32)
    y = xf * lax.rsqrt(jnp.mean(xf * xf, axis=-1, keepdims=True) + EPS)
    return (y * g.astype(jnp.float32)).astype(x.dtype)

def neighbourhood_attention(q, k, v, rpb):
    B, S, H, Dh = q.shape
    rows = S // GRID_W
    kr = min(NA_KR_MAX, rows)

    def to_grid(t):
        return t.reshape(B, rows, GRID_W, H, Dh).transpose(0, 3, 1, 2, 4)

    qg, kg, vg = to_grid(q), to_grid(k), to_grid(v)
    r = jnp.arange(rows)
    r0 = jnp.clip(r - kr // 2, 0, rows - kr)
    row_idx = r0[:, None] + jnp.arange(kr)[None, :]
    c = jnp.arange(GRID_W)
    c0 = jnp.clip(c - NA_KW // 2, 0, GRID_W - NA_KW)
    col_in = (c[None, :] >= c0[:, None]) & (c[None, :] < c0[:, None] + NA_KW)

    k_rows = kg[:, :, row_idx]
    v_rows = vg[:, :, row_idx]
    s = jnp.einsum('bhrqd,bhrjkd->bhrqjk', qg, k_rows).astype(jnp.float32) * (Dh ** -0.5)

    dr_idx = row_idx - r[:, None] + (NA_KR_MAX - 1)
    dc_idx = jnp.clip(c[None, :] - c[:, None] + (NA_KW - 1), 0, 2 * NA_KW - 2)
    bias = rpb.astype(jnp.float32)[:, dr_idx[:, None, :, None], dc_idx[None, :, None, :]]
    s = s + bias[None]
    s = jnp.where(col_in[:, None, :], s, -jnp.inf)
    p = jax.nn.softmax(s.reshape(B, H, rows, GRID_W, kr * GRID_W), axis=-1)
    p = p.reshape(B, H, rows, GRID_W, kr, GRID_W).astype(v.dtype)
    o = jnp.einsum('bhrqjk,bhrjkd->bhrqd', p, v_rows)
    return o.transpose(0, 2, 3, 1, 4).reshape(B, S, H * Dh)

def short_conv(u, w, b):
    up = jnp.pad(u, ((0, 0), (1, 1), (0, 0)))
    return up[:, :-2] * w[0] + up[:, 1:-1] * w[1] + up[:, 2:] * w[2] + b

def hyena_pos_features(L):
    t = jnp.linspace(0.0, 1.0, L, dtype=jnp.float32)[:, None]
    w = 2.0 * math.pi * jnp.arange(L, dtype=jnp.float32)[:, None] / L
    f = jnp.linspace(1e-4, HY_POS_BANDS - 1, HY_POS_BANDS, dtype=jnp.float32)[None, :]
    return jnp.concatenate([t, jnp.cos(f * w), -jnp.sin(f * w)], axis=-1), t

def hyena_filters(z, t, w1, b1, freq, w2, b2, w3):
    f32 = jnp.float32
    fr = freq.astype(f32)
    h = jnp.sin(fr * (z @ w1.astype(f32) + b1.astype(f32)))
    h = jnp.sin(fr * (h @ w2.astype(f32) + b2.astype(f32)))
    h = h @ w3.astype(f32)
    max_decay = math.log(HY_DECAY_TARGET) / HY_FAST_PCT
    min_decay = math.log(HY_DECAY_TARGET) / HY_SLOW_PCT
    deltas = jnp.linspace(min_decay, max_decay, HY_WIDTH, dtype=f32)
    decay = jnp.exp(-t * jnp.abs(deltas)[None, :])
    h = h.reshape(-1, 2, HY_WIDTH) * decay[:, None, :]
    return h[:, 0], h[:, 1]

def fft_conv(u, h):
    L = u.shape[1]
    n = 2 * L
    U = jnp.fft.rfft(u, n=n, axis=1)
    Hf = jnp.fft.rfft(h, n=n, axis=0)
    return jnp.fft.irfft(U * Hf[None], n=n, axis=1)[:, :L]

def hyena_mixer(u, h_fwd, h_bwd, skip_bias):
    x0, x1, vv = jnp.split(u.astype(jnp.float32), 3, axis=-1)
    z = vv * x1
    y = (fft_conv(z, h_fwd)
         + jnp.flip(fft_conv(jnp.flip(z, axis=1), h_bwd), axis=1)
         + z * skip_bias.astype(jnp.float32))
    return (y * x0).astype(u.dtype)

def peer(h, wq, subkeys, u_tab, v_tab):
    B, S, D = h.shape
    T = B * S
    half = PEER_DKEY // 2

    def chunk(xc):
        C = xc.shape[0]
        q = (xc @ wq).reshape(C, PEER_HEADS, 2, half)
        s = jnp.einsum('thpd,hpkd->thpk', q, subkeys).astype(jnp.float32)
        sv, si = lax.top_k(s, PEER_TOPK)
        cand = (sv[:, :, 0, :, None] + sv[:, :, 1, None, :]).reshape(C, PEER_HEADS, PEER_TOPK * PEER_TOPK)
        cid = (si[:, :, 0, :, None] * PEER_NKEYS + si[:, :, 1, None, :]).reshape(C, PEER_HEADS, PEER_TOPK * PEER_TOPK)
        fs, fi = lax.top_k(cand, PEER_TOPK)
        eid = jnp.take_along_axis(cid, fi, axis=-1)
        g = jax.nn.softmax(fs, axis=-1)
        u = u_tab[eid]
        a = jax.nn.gelu(jnp.einsum('tc,thkc->thk', xc, u).astype(jnp.float32))
        vg = v_tab[eid]
        return jnp.einsum('thk,thkc->tc', (g * a).astype(xc.dtype), vg)

    out = lax.map(chunk, h.reshape(T // PEER_CHUNK, PEER_CHUNK, D))
    return out.reshape(B, S, D)

def setup_inputs(seed: int = 0) -> dict:
    key = jax.random.key(seed)
    ks = iter(jax.random.split(key, 32))

    def nrm(shape, scale):
        return jax.random.normal(next(ks), shape, jnp.float32) * scale

    return {
        "x": nrm((BATCH, SEQ, D_MODEL), 1.0),
        "norm1_g": 1.0 + nrm((DEPTH, D_MODEL), 0.02),
        "w_in": nrm((DEPTH, D_MODEL, IN_WIDTH), D_MODEL ** -0.5),
        "gate_b": nrm((DEPTH, N_BRANCHES, D_MODEL), 0.02),
        "na_q_g": 1.0 + nrm((DEPTH, NA_HEAD_DIM), 0.02),
        "na_k_g": 1.0 + nrm((DEPTH, NA_HEAD_DIM), 0.02),
        "na_rpb": nrm((DEPTH, NA_HEADS, 2 * NA_KR_MAX - 1, 2 * NA_KW - 1), 0.02),
        "hy_conv_w": nrm((DEPTH, HY_SHORT, 3 * HY_WIDTH), HY_SHORT ** -0.5),
        "hy_conv_b": nrm((DEPTH, 3 * HY_WIDTH), 0.02),
        "hy_w1": nrm((DEPTH, HY_POS_DIM, HY_FFN_HIDDEN), HY_POS_DIM ** -0.5),
        "hy_b1": nrm((DEPTH, HY_FFN_HIDDEN), 0.02),
        "hy_freq": 1.0 + nrm((DEPTH, HY_FFN_HIDDEN), 0.02),
        "hy_w2": nrm((DEPTH, HY_FFN_HIDDEN, HY_FFN_HIDDEN), HY_FFN_HIDDEN ** -0.5),
        "hy_b2": nrm((DEPTH, HY_FFN_HIDDEN), 0.02),
        "hy_w3": nrm((DEPTH, HY_FFN_HIDDEN, 2 * HY_WIDTH), HY_FILTER_SCALE * HY_FFN_HIDDEN ** -0.5),
        "hy_bias": nrm((DEPTH, HY_WIDTH), 1.0),
        "w_up_na": nrm((DEPTH, NA_WIDTH, D_MODEL), NA_WIDTH ** -0.5),
        "w_up_hy": nrm((DEPTH, HY_WIDTH, D_MODEL), HY_WIDTH ** -0.5),
        "w_out": nrm((DEPTH, D_MODEL, D_MODEL), D_MODEL ** -0.5),
        "norm2_g": 1.0 + nrm((DEPTH, D_MODEL), 0.02),
        "peer_wq": nrm((DEPTH, D_MODEL, PEER_HEADS * PEER_DKEY), D_MODEL ** -0.5),
        "peer_subkeys": nrm((DEPTH, PEER_HEADS, 2, PEER_NKEYS, PEER_DKEY // 2), (PEER_DKEY // 2) ** -0.5),
        "peer_u": nrm((DEPTH, PEER_N, D_MODEL), D_MODEL ** -0.5),
        "peer_v": nrm((DEPTH, PEER_N, D_MODEL), D_MODEL ** -0.5),
    }

def reference(x, norm1_g, w_in, gate_b, na_q_g, na_k_g, na_rpb, hy_conv_w, hy_conv_b,
              hy_w1, hy_b1, hy_freq, hy_w2, hy_b2, hy_w3, hy_bias, w_up_na, w_up_hy,
              w_out, norm2_g, peer_wq, peer_subkeys, peer_u, peer_v):
    B, S, D = x.shape
    pos_z, pos_t = hyena_pos_features(S)
    splits = [NA_WIDTH, 2 * NA_WIDTH, 3 * NA_WIDTH, 3 * NA_WIDTH + 3 * HY_WIDTH]
    for l in range(DEPTH):
        hn = rmsnorm(x, norm1_g[l])
        proj = hn @ w_in[l]
        q, k, v, hy_in, gates = jnp.split(proj, splits, axis=-1)
        q = rmsnorm(q.reshape(B, S, NA_HEADS, NA_HEAD_DIM), na_q_g[l])
        k = rmsnorm(k.reshape(B, S, NA_HEADS, NA_HEAD_DIM), na_k_g[l])
        v = v.reshape(B, S, NA_HEADS, NA_HEAD_DIM)
        a_out = neighbourhood_attention(q, k, v, na_rpb[l])

        u = short_conv(hy_in, hy_conv_w[l], hy_conv_b[l])
        h_fwd, h_bwd = hyena_filters(pos_z, pos_t, hy_w1[l], hy_b1[l], hy_freq[l],
                                     hy_w2[l], hy_b2[l], hy_w3[l])
        b_out = hyena_mixer(u, h_fwd, h_bwd, hy_bias[l])

        g = jax.nn.sigmoid((gates.reshape(B, S, N_BRANCHES, D) + gate_b[l]).astype(jnp.float32)).astype(x.dtype)
        merged = g[:, :, 0] * (a_out @ w_up_na[l]) + g[:, :, 1] * (b_out @ w_up_hy[l])
        x = x + merged @ w_out[l]
        x = x + peer(rmsnorm(x, norm2_g[l]), peer_wq[l], peer_subkeys[l], peer_u[l], peer_v[l])
    return x


_drawn_inputs = setup_inputs


def setup_inputs(seed=0):
    import zlib

    import numpy as np

    out = dict(_drawn_inputs(seed))
    spreads = {}
    factors = {'gate_b': 8.0,
     'na_q_g': 8.0,
     'na_k_g': 8.0,
     'na_rpb': 8.0,
     'hy_b1': 8.0,
     'hy_freq': 8.0,
     'hy_b2': 8.0,
     'norm2_g': 8.0,
     'peer_wq': 2.918,
     'peer_subkeys': 2.918,
     'peer_u': 3.248,
     'peer_v': 2.905}
    for name, (base, spread) in spreads.items():
        noise = np.random.default_rng([zlib.crc32(name.encode()), seed]).standard_normal(out[name].shape)
        drawn = base * np.exp(spread * noise) if base else spread * noise
        out[name] = __import__('jax').numpy.asarray(drawn.astype(out[name].dtype))
    for name, factor in factors.items():
        out[name] = (out[name] * factor).astype(out[name].dtype)
    return out
```

```python
import math
from contextlib import ExitStack

import numpy as np

import concourse.bass as bass
from concourse import mybir
from concourse.alu_op_type import AluOpType as ALU

P = 128
D = 1024
S = 256
DEPTH = 2
GRID_W = 64
ROWS = S // GRID_W
NH = 8
HD = 64
KR_MAX = 8
KW = 16
HW = 512
BANDS = 16
POS = 1 + 2 * BANDS
FFN = 64
PH = 8
NK = 128
TOPK = 16
EPS = 1e-6

KT = D // P
TT = S // P
RING = 8
T_QK, T_V, T_HY, T_GATE = 0, 8, 12, 24
T_UP, T_OUT, T_WQ, T_U = 40, 48, 56, 72
T_VT = T_U + NK
TILES = T_VT + NK
GROUPS = TILES // RING
HALF = NK // 2
TOK = S // HALF

C_G1, C_G2, C_GB, C_QG, C_KG, C_CW, C_CB = 0, 8, 16, 32, 33, 34, 70
N_COLS = 82

F32 = mybir.dt.float32
BF16 = mybir.dt.bfloat16
U32 = mybir.dt.uint32
ACT = mybir.ActivationFunctionType
AX = mybir.AxisListType.X
LOWEST = -3.0e38
MAGIC = 1.5 * 2.0 ** 23
TWO_PI_HI = 6.28125
TWO_PI_LO = 2.0 * math.pi - TWO_PI_HI
PI_BELOW = 3.1415925


class Signal:

    def __init__(self, sem, per_layer):
        self.sem, self.per_layer = sem, per_layer

    def at(self, layer, count):
        return layer * self.per_layer + count


def encoder_kernel(nc, x_in, stream, subkeys, cols, ffn_cols, w1_in, w2_in, w3_in, skip_in, rpb_in,
                   pos_in, dft_in, decay_in, mask_in, mats_in, iota_in, out):
    ctx = ExitStack()
    with ctx:
        def sb(name, shape, dt=F32):
            return ctx.enter_context(nc.sbuf_tensor(name, shape, dt))

        def sem(name):
            return ctx.enter_context(nc.semaphore(name))

        def sig(name, per_layer):
            return Signal(sem(name), per_layer)

        arena = sb("arena", [P, NK * S])
        ring = sb("ring", [P, RING, D])
        xT = sb("xT", [P, KT, S])
        hT = sb("hT", [P, KT, S])
        mats = sb("mats", [P, 3, P])
        iota = sb("iota", [P, P])
        iota_k = sb("iota_k", [P, TOPK])
        eps_col = sb("eps_col", [P, 1])
        zeros = sb("zeros", [P, 512], BF16)
        all_cols = sb("all_cols", [P, DEPTH, N_COLS])
        col = sb("col", [P, N_COLS])
        half_gate_b = sb("half_gate_b", [P, 16])
        norm_tmp = sb("norm_tmp", [P, 3, 512])
        soft = sb("soft", [P, 2, 3, TT])
        slotT = sb("slotT", [P, 3, S])
        onehot_i = sb("onehot_i", [P, TOK, NK])
        onehot_j = sb("onehot_j", [P, TOK, HALF])
        spectrum = sb("spectrum", [P, 2, TT, HW])
        bank = [ctx.enter_context(nc.psum_tensor(f"bank{i}", [P, 512], F32)) for i in range(8)]

        identity, mean_all, mean_head = mats[:, 0, :], mats[:, 1, :], mats[:, 2, :]
        experts = arena[:, :].rearrange("p (j t) -> p j t", t=S)

        def part(kb, *dims, dt=F32):
            n = int(np.prod(dims))
            v = arena[:, int(kb * 256):int(kb * 256) + n]
            if dt != F32:
                v = v.bitcast(dt)
            names = "abcd"[:len(dims)]
            if len(dims) > 1:
                sizes = {c: d for c, d in zip(names[1:], dims[1:])}
                v = v.rearrange(f"p ({' '.join(names)}) -> p {' '.join(names)}", **sizes)
            return v

        squares = part(0, KT, S)
        merged = part(0, KT, S)
        qk_raw = part(8, 8, S)
        zT = part(8, 4, S)
        z_tok = part(12, TT, HW)
        qk_sq = part(16, 8, S)
        attn_T = part(16, 4, S)
        hyena_T = part(20, 4, S)
        qk_n = part(24, 8, S)
        v_tok = part(32, TT, HW)
        u_pad = part(36, 12, S + 2)
        prod = part(36, 2, HW)
        u = part(49, 12, S)
        gates = part(61, 16, S)
        h1, h2, arg, turns = part(61, S), part(62, S), part(63, S), part(64, S)
        w3 = part(65, 2, HW)
        w3_sd = part(69, 2, HW)
        w1 = part(73, FFN)
        w2 = part(73.25, FFN)
        ffn_col = part(73.5, 4)
        bias = part(77, NH, TT, S)
        scores = part(93, 2, TT, S)
        probs = part(97, 2, TT, S)
        probs_T = part(101, 2, TT, S)
        dft = part(105, 4, TT, S)
        decay = part(113, TT, HW)
        mask = part(117, S)
        pos = part(118, S)
        filters = part(119, 2, TT, HW)
        spec_y = part(119, 2, TT, HW)
        q2T = part(24, 2 * PH, S)
        subk = part(40, 2 * PH, NK)
        s_all = part(64, TT, 2 * PH * NK)
        s_cur = part(80, 2 * PH, NK)
        s_rest = part(88, 2 * PH, NK)
        cand = part(96, PH, TOPK, TOPK)
        cand_rest = part(104, PH, TOPK * TOPK)
        pick = part(112, PH * TOPK, TOPK)
        top_s = part(120, 2 * PH, TOPK)
        top_i = part(121, 2 * PH, TOPK, dt=U32)
        top_if = part(122, PH, 2, TOPK)
        best_s = part(123, PH * TOPK)
        best_i = part(123.5, PH, TOPK, dt=U32)
        rank = part(124, 2, PH * TOPK, dt=U32)
        rank_f = part(125, 2, PH * TOPK)
        best_all = part(126, TT, PH * TOPK)
        expd = part(127, TT, PH * TOPK)
        slots = norm_tmp[:, :, :].rearrange("p a b -> p (a b)")[:, 0:TT * 3 * P].rearrange(
            "p (t c s) -> p t c s", t=TT, c=3)

        consts_in = sem("consts_in")
        x_loaded = sem("x_loaded")
        small_in = sig("small_in", 16 * (9 + ROWS))
        subk_in = sig("subk_in", 16)
        ring_full = [sig(f"ring_full{s}", 16 * GROUPS) for s in range(RING)]
        tile_done = sig("tile_done", TILES)
        layer_open = sem("layer_open")
        setup_done = sig("setup_done", 1)
        sq_ready = sig("sq_ready", 2)
        ms_done = sig("ms_done", 2)
        y0_ready = sig("y0_ready", 2)
        h_ready = sig("h_ready", 2)
        ffn_done = sig("ffn_done", 2)
        arg_ready = sig("arg_ready", 2)
        sin_done = sig("sin_done", 2)
        tile_copied = sig("tile_copied", 52)
        v_ready = sig("v_ready", 2)
        ss_done = sig("ss_done", 4)
        qk_y0 = sig("qk_y0", 4)
        qk_ready = sig("qk_ready", 4)
        w3_ready = sig("w3_ready", 1)
        taps_done = sig("taps_done", 4)
        filters_ready = sig("filters_ready", 4)
        spec_done = sig("spec_done", 4)
        spec_ready = sig("spec_ready", 4)
        scores_done = sig("scores_done", NH)
        scores_ready = sig("scores_ready", NH)
        exp_done = sig("exp_done", NH)
        probs_ready = sig("probs_ready", NH)
        pT_done = sig("pT_done", NH)
        pT_ready = sig("pT_ready", NH)
        pv_done = sig("pv_done", NH)
        attn_ready = sig("attn_ready", NH // 2)
        z_ready = sig("z_ready", 1)
        zt_done = sig("zt_done", TT)
        zt_ready = sig("zt_ready", TT)
        zf_done = sig("zf_done", TT)
        y_ready = sig("y_ready", TT)
        conv_done = sig("conv_done", 4)
        hyena_ready = sig("hyena_ready", 4)
        up_used = sig("up_used", 8)
        out_used = sig("out_used", 8)
        score_done = sig("score_done", 8)
        score_copied = sig("score_copied", 8)
        gelu_done = sig("gelu_done", NK)
        best_ready = sig("best_ready", 1)
        expd_ready = sig("expd_ready", 1)
        slots_ready = sig("slots_ready", 1)
        slotT_done = sig("slotT_done", TT)
        route_done = sig("route_done", 1)
        onehot_ready = sig("onehot_ready", 2 * HALF)
        g_done = sig("g_done", 2 * HALF)
        g_used = sig("g_used", 2 * HALF)
        acc_closed = sig("acc_closed", 1)
        act_chain = sem("act_chain")
        dve_chain = sem("dve_chain")
        route_chain = sem("route_chain")
        onehot_chain = sem("onehot_chain")
        stored = sem("stored")

        block = ctx.enter_context(nc.Block())

        @block.sync
        def _(sp):
            def load(n, slot):
                sp.dma_start(ring[:, slot, :], stream[bass.ds(n, 1), :, :].rearrange("a p n -> (a p) n")
                             ).then_inc(ring_full[slot].sem, 16)

            for slot in range(RING):
                load(slot, slot)
            with sp.Fori(1, DEPTH * GROUPS) as turn:
                for slot in range(RING):
                    sp.wait_ge(tile_done.sem, turn * RING + (slot + 1 - RING))
                    load(turn * RING + slot, slot)
            sp.wait_ge(layer_open, DEPTH + 1)
            sp.dma_start(out, xT[:, :, :]).then_inc(stored, 16)
            sp.wait_ge(stored, 16)

        @block.gpsimd
        def _(pool):
            def load(dst, src, s):
                pool.dma_start(dst, src).then_inc(s, 16)

            with pool.Fori(0, DEPTH) as l:
                pool.wait_ge(layer_open, l + 1)
                at = bass.ds(l, 1)
                s = small_in.sem
                load(w1[0:POS, :], w1_in[at].rearrange("a p n -> (a p) n"), s)
                load(w2[0:FFN, :], w2_in[at].rearrange("a p n -> (a p) n"), s)
                load(w3[0:FFN, :, :], w3_in[at].rearrange("a p b n -> (a p) b n"), s)
                load(ffn_col[0:FFN, 0:3], ffn_cols[at].rearrange("a p n -> (a p) n"), s)
                load(part(74, HW)[0:1, :], skip_in[at, :], s)
                load(pos[0:POS, :], pos_in, s)
                load(dft[:, :, :, :], dft_in, s)
                load(decay[:, :, :], decay_in, s)
                load(mask, mask_in, s)
                for r in range(ROWS):
                    qt, p0 = r // 2, (r % 2) * GRID_W
                    load(bias[p0:p0 + GRID_W, :, qt, :].rearrange("c h (k n) -> c h k n", k=ROWS),
                         rpb_in[at, :, :, ROWS - 1 - r:2 * ROWS - 1 - r, :].rearrange(
                             "a c h k n -> (a c) h k n"), s)
                pool.wait_ge(hyena_ready.sem, hyena_ready.at(l, 4))
                load(subk[:, :, :], subkeys[at].rearrange("a p m n -> (a p) m n"), subk_in.sem)

        @block.scalar
        def _(act):
            steps = [0]

            act.dma_start(xT[:, :, :], x_in).then_inc(x_loaded, 16)
            act.dma_start(mats[:, :, :], mats_in).then_inc(consts_in, 16)
            act.dma_start(iota[:, :], iota_in).then_inc(consts_in, 16)
            act.dma_start(all_cols[:, :, :], cols).then_inc(consts_in, 16)

            with act.Fori(0, DEPTH) as l:
                act.drain()
                act.sem_clear(act_chain)

                def link(ins):
                    steps[0] += 1
                    ins.then_inc(act_chain, 1)
                    act.wait_ge(act_chain, steps[0])

                def rsqrt_guess(src, n, done):
                    link(nc.scalar.activation(norm_tmp[:, 1, 0:n], src, ACT.Ln, bias=eps_col[:, :]))
                    nc.scalar.activation(norm_tmp[:, 0, 0:n], norm_tmp[:, 1, 0:n], ACT.Exp,
                                         scale=-0.5).then_inc(done, 1)

                def tile_wait(tile):
                    act.wait_ge(tile_done.sem, tile_done.at(l, tile + 1))

                def copy_tile(tile, m, dst):
                    tile_wait(tile)
                    nc.scalar.activation(dst, bank[m % 4][:, 0:S], ACT.Copy).then_inc(tile_copied.sem, 1)

                def norm(n):
                    nc.scalar.activation(squares[:, :, :], xT[:, :, :], ACT.Square).then_inc(sq_ready.sem, 1)
                    act.wait_ge(ms_done.sem, ms_done.at(l, n))
                    rsqrt_guess(bank[4][:, 0:S], S, y0_ready.sem)

                act.wait_ge(layer_open, l + 1)
                act.wait_ge(setup_done.sem, setup_done.at(l, 1))
                norm(1)
                act.wait_ge(arg_ready.sem, arg_ready.at(l, 1))
                nc.scalar.activation(h1[0:FFN, :], arg[0:FFN, :], ACT.Sin).then_inc(sin_done.sem, 1)
                for m in range(8):
                    tile_wait(T_QK + m)
                    nc.scalar.activation(qk_raw[:, m, :], bank[m % 4][:, 0:S], ACT.Copy)
                    nc.scalar.activation(qk_sq[:, m, :], bank[m % 4][:, 0:S], ACT.Square
                                         ).then_inc(tile_copied.sem, 1)
                act.wait_ge(arg_ready.sem, arg_ready.at(l, 2))
                nc.scalar.activation(h2[0:FFN, :], arg[0:FFN, :], ACT.Sin).then_inc(sin_done.sem, 1)
                tile_wait(T_V + 3)
                for tt in range(TT):
                    nc.scalar.activation(v_tok[:, tt, :], bank[6 + tt][:, :], ACT.Copy).then_inc(v_ready.sem, 1)
                for n in range(4):
                    copy_tile(T_HY + n, 8 + n, u_pad[:, n, 1:S + 1])
                for n in range(4):
                    act.wait_ge(ss_done.sem, ss_done.at(l, n + 1))
                    if n:
                        act.wait_ge(qk_ready.sem, qk_ready.at(l, n))
                    rsqrt_guess(bank[4 + n % 2][:, :], 512, qk_y0.sem)
                for n in range(4, 12):
                    copy_tile(T_HY + n, 8 + n, u_pad[:, n, 1:S + 1])
                for n in range(4):
                    act.wait_ge(spec_done.sem, spec_done.at(l, n + 1))
                    nc.scalar.activation(spectrum[:, n // TT, n % TT, :], bank[4 + n][:, :], ACT.Copy
                                         ).then_inc(spec_ready.sem, 1)

                def gate(m):
                    tile_wait(T_GATE + m)
                    nc.scalar.activation(gates[:, m, :], bank[m % 4][:, 0:S], ACT.Tanh, scale=0.5,
                                         bias=half_gate_b[:, m:m + 1]).then_inc(tile_copied.sem, 1)

                def head_exp(h):
                    act.wait_ge(scores_ready.sem, scores_ready.at(l, h + 1))
                    for qt in range(TT):
                        last = nc.scalar.activation(probs[:, h % 2, qt, :], scores[:, h % 2, qt, :], ACT.Exp,
                                                    bias=soft[:, h % 2, 0, qt:qt + 1],
                                                    accum_out=soft[:, h % 2, 1, qt:qt + 1])
                        if qt == 0:
                            link(last)
                    last.then_inc(exp_done.sem, 1)

                head_exp(0)
                head_exp(1)
                for h in range(NH):
                    gate(2 * h)
                    act.wait_ge(pT_done.sem, pT_done.at(l, h + 1))
                    nc.scalar.activation(probs_T[:, h % 2, :, :], bank[6][:, :].rearrange(
                        "p (k q) -> p k q", k=TT), ACT.Copy).then_inc(pT_ready.sem, 1)
                    gate(2 * h + 1)
                    if h + 2 < NH:
                        head_exp(h + 2)
                for tt in range(TT):
                    act.wait_ge(zt_done.sem, zt_done.at(l, tt + 1))
                    nc.scalar.activation(z_tok[:, tt, :], bank[4 + tt][:, :], ACT.Copy).then_inc(zt_ready.sem, 1)
                act.wait_ge(out_used.sem, out_used.at(l, 8))
                norm(2)
                with act.Fori(0, 2) as w:
                    for s in range(RING):
                        act.wait_ge(tile_done.sem, tile_done.at(l, w * RING + (T_WQ + s + 1)))
                        nc.scalar.activation(q2T[:, bass.ds(w * RING + s, 1), :].rearrange("p a t -> p (a t)"),
                                             bank[s % 4][:, 0:S], ACT.Copy).then_inc(tile_copied.sem, 1)
                for n in range(8):
                    tt, g = n // 4, n % 4
                    act.wait_ge(score_done.sem, score_done.at(l, n + 1))
                    nc.scalar.activation(s_all[:, tt, g * 512:(g + 1) * 512], bank[4 + g][:, :], ACT.Copy
                                         ).then_inc(score_copied.sem, 1)

                def gelus(first, count):
                    with act.Fori(0, count // RING) as i:
                        for s in range(RING):
                            act.wait_ge(tile_done.sem, tile_done.at(l, i * RING + (T_U + first + s + 1)))
                            nc.scalar.activation(experts[:, bass.ds(i * RING + (first + s), 1), :].rearrange(
                                "p a t -> p (a t)"), bank[s % 2][:, 0:S], ACT.Gelu_apprx_tanh
                                ).then_inc(gelu_done.sem, 1)

                gelus(0, 48)
                act.wait_ge(best_ready.sem, best_ready.at(l, 1))
                nc.scalar.activation(expd[:, :, :], expd[:, :, :], ACT.Exp).then_inc(expd_ready.sem, 1)
                gelus(48, 16)
                act.wait_ge(route_done.sem, route_done.at(l, 1))
                gelus(64, 64)

        @block.vector
        def _(dve):
            count = [0]
            V = nc.vector
            V.memset(zeros[:, :], 0.0)
            V.memset(eps_col[:, :], EPS)
            dve.wait_ge(consts_in, 48)
            V.tensor_copy(iota_k[:, :], iota[:, 0:TOPK])
            dve.wait_ge(x_loaded, 16)
            V.drain().then_inc(layer_open, 1)

            with dve.Fori(0, DEPTH) as l:
                dve.drain()
                dve.sem_clear(dve_chain)

                def link(ins):
                    count[0] += 1
                    ins.then_inc(dve_chain, 1)
                    dve.wait_ge(dve_chain, count[0])

                def refine(src, n):
                    y0, t, y = norm_tmp[:, 0, 0:n], norm_tmp[:, 1, 0:n], norm_tmp[:, 2, 0:n]
                    link(V.tensor_tensor(t, y0, y0, ALU.mult))
                    link(V.scalar_tensor_tensor(t, src, EPS, t, ALU.add, ALU.mult))
                    link(V.tensor_scalar(t, t, -0.5, 1.5, ALU.mult, ALU.add))
                    link(V.tensor_tensor(y, y0, t, ALU.mult))

                def norm(n, gain):
                    dve.wait_ge(y0_ready.sem, y0_ready.at(l, n))
                    refine(bank[4][:, 0:S], S)
                    for k in range(KT):
                        last = V.scalar_tensor_tensor(hT[:, k, :], xT[:, k, :], col[:, gain + k:gain + k + 1],
                                                      norm_tmp[:, 2, 0:S], ALU.mult, ALU.mult)
                    last.then_inc(h_ready.sem, 1)

                def sine_argument(n, b):
                    f = slice(0, FFN)
                    dve.wait_ge(ffn_done.sem, ffn_done.at(l, n))
                    link(V.tensor_scalar(arg[f, :], bank[5][f, 0:S], ffn_col[f, b:b + 1], ffn_col[f, 1:2],
                                         ALU.add, ALU.mult))
                    link(V.tensor_scalar(turns[f, :], arg[f, :], 1.0 / (2.0 * math.pi), MAGIC, ALU.mult, ALU.add))
                    link(V.tensor_scalar(turns[f, :], turns[f, :], MAGIC, None, ALU.subtract))
                    link(V.scalar_tensor_tensor(arg[f, :], turns[f, :], -TWO_PI_HI, arg[f, :], ALU.mult, ALU.add))
                    link(V.scalar_tensor_tensor(arg[f, :], turns[f, :], -TWO_PI_LO, arg[f, :], ALU.mult, ALU.add))
                    V.tensor_scalar(arg[f, :], arg[f, :], PI_BELOW, -PI_BELOW, ALU.min, ALU.max
                                    ).then_inc(arg_ready.sem, 1)

                V.tensor_copy(col[:, :], all_cols[:, bass.ds(l, 1), :].rearrange("p a n -> p (a n)"))
                V.tensor_scalar(half_gate_b[:, :], all_cols[:, bass.ds(l, 1), C_GB:C_GB + 16].rearrange(
                    "p a n -> p (a n)"), 0.5, None, ALU.mult)
                V.memset(u_pad[:, :, 0:1], 0.0)
                V.memset(u_pad[:, :, S + 1:S + 2], 0.0).then_inc(setup_done.sem, 1)
                dve.wait_ge(small_in.sem, small_in.at(l, small_in.per_layer))
                f = slice(0, FFN)
                V.tensor_tensor(w3_sd[f, 0, :], w3[f, 0, :], w3[f, 1, :], ALU.add)
                V.tensor_tensor(w3_sd[f, 1, :], w3[f, 0, :], w3[f, 1, :], ALU.subtract
                                ).then_inc(w3_ready.sem, 1)
                norm(1, C_G1)
                sine_argument(1, 0)
                dve.wait_ge(sin_done.sem, sin_done.at(l, 1))
                sine_argument(2, 2)

                for n in range(4):
                    dve.wait_ge(qk_y0.sem, qk_y0.at(l, n + 1))
                    refine(bank[4 + n % 2][:, :], 512)
                    gain = C_QG if n < 2 else C_KG
                    V.scalar_tensor_tensor(qk_n[:, 2 * n:2 * n + 2, :].rearrange("p a t -> p (a t)"),
                                           qk_raw[:, 2 * n:2 * n + 2, :].rearrange("p a t -> p (a t)"),
                                           col[:, gain:gain + 1], norm_tmp[:, 2, :], ALU.mult, ALU.mult
                                           ).then_inc(qk_ready.sem, 1)
                for n in range(4):
                    sd, tt = n // TT, n % TT
                    dve.wait_ge(taps_done.sem, taps_done.at(l, n + 1))
                    ins = V.tensor_tensor(filters[:, sd, tt, :], bank[4 + n][:, :], decay[:, tt, :], ALU.mult)
                    if n == 0:
                        link(ins)
                        ins = V.tensor_tensor(filters[0:1, 0, 0, :], filters[0:1, 0, 0, :],
                                              part(74, HW)[0:1, :], ALU.add)
                    ins.then_inc(filters_ready.sem, 1)
                for h in range(NH):
                    ins = V.tensor_tensor(bias[:, h, :, :], bias[:, h, :, :],
                                          mask.unsqueeze(1).to_broadcast([P, TT, S]), ALU.add)
                link(ins)

                def conv(n):
                    if n % 4 == 0:
                        dve.wait_ge(tile_copied.sem, tile_copied.at(l, 8 + n + 4))
                    w = C_CW + 3 * n
                    link(V.tensor_scalar(u[:, n, :], u_pad[:, n, 1:S + 1], col[:, w + 1:w + 2],
                                         col[:, C_CB + n:C_CB + n + 1], ALU.mult, ALU.add))
                    link(V.scalar_tensor_tensor(u[:, n, :], u_pad[:, n, 0:S], col[:, w:w + 1], u[:, n, :],
                                                ALU.mult, ALU.add))
                    link(V.scalar_tensor_tensor(u[:, n, :], u_pad[:, n, 2:S + 2], col[:, w + 2:w + 3], u[:, n, :],
                                                ALU.mult, ALU.add))

                def head_scores(h):
                    dve.wait_ge(scores_done.sem, scores_done.at(l, h + 1))
                    link(V.scalar_tensor_tensor(scores[:, h % 2, :, :].rearrange("p a t -> p (a t)"),
                                                bank[4 + h % 2][:, :], HD ** -0.5,
                                                bias[:, h, :, :].rearrange("p a t -> p (a t)"),
                                                ALU.mult, ALU.add))
                    V.tensor_reduce(soft[:, h % 2, 0, :], scores[:, h % 2, :, :], AX, ALU.max, negate=True
                                    ).then_inc(scores_ready.sem, 1)

                head_scores(0)
                head_scores(1)
                tiles = list(range(12))
                for h in range(NH):
                    dve.wait_ge(exp_done.sem, exp_done.at(l, h + 1))
                    link(V.reciprocal(soft[:, h % 2, 2, :], soft[:, h % 2, 1, :]))
                    for qt in range(TT):
                        ins = V.tensor_scalar(probs[:, h % 2, qt, :], probs[:, h % 2, qt, :],
                                              soft[:, h % 2, 2, qt:qt + 1], None, ALU.mult)
                        if qt == 0:
                            link(ins)
                    ins.then_inc(probs_ready.sem, 1)
                    for _ in range(2 - h % 2):
                        conv(tiles.pop(0))
                    if h + 2 < NH:
                        head_scores(h + 2)
                    if h % 2:
                        dve.wait_ge(pv_done.sem, pv_done.at(l, h + 1))
                        V.tensor_copy(attn_T[:, h // 2, :], bank[7][:, 0:S]).then_inc(attn_ready.sem, 1)
                V.tensor_tensor(zT[:, :, :], u[:, 4:8, :], u[:, 8:12, :], ALU.mult).then_inc(z_ready.sem, 1)
                for f in range(TT):
                    re, im = (bank[6], bank[7]) if f == 0 else (bank[4], bank[5])
                    dve.wait_ge(zf_done.sem, zf_done.at(l, f + 1))
                    if f:
                        dve.wait_ge(y_ready.sem, y_ready.at(l, f))
                    V.tensor_tensor(prod[:, 0, :], re[:, :], spectrum[:, 0, f, :], ALU.mult)
                    link(V.tensor_tensor(prod[:, 1, :], im[:, :], spectrum[:, 1, f, :], ALU.mult))
                    link(V.tensor_tensor(spec_y[:, 0, f, :], prod[:, 0, :], prod[:, 1, :], ALU.subtract))
                    V.tensor_tensor(prod[:, 0, :], re[:, :], spectrum[:, 1, f, :], ALU.mult)
                    link(V.tensor_tensor(prod[:, 1, :], im[:, :], spectrum[:, 0, f, :], ALU.mult))
                    V.tensor_tensor(spec_y[:, 1, f, :], prod[:, 0, :], prod[:, 1, :], ALU.add
                                    ).then_inc(y_ready.sem, 1)
                for ct in range(4):
                    dve.wait_ge(conv_done.sem, conv_done.at(l, 4))
                    V.tensor_tensor(hyena_T[:, ct, :], bank[6 + ct // 2][:, (ct % 2) * S:(ct % 2 + 1) * S],
                                    u[:, ct, :], ALU.mult).then_inc(hyena_ready.sem, 1)
                for m in range(8):
                    dve.wait_ge(tile_done.sem, tile_done.at(l, T_UP + m + 1))
                    b = bank[m % 4]
                    link(V.scalar_tensor_tensor(merged[:, m, :], gates[:, m, :], 1.0, b[:, 0:S], ALU.add, ALU.mult))
                    link(V.scalar_tensor_tensor(prod[:, 0, 0:S], gates[:, 8 + m, :], 1.0, b[:, S:2 * S],
                                                ALU.add, ALU.mult))
                    V.tensor_tensor(merged[:, m, :], merged[:, m, :], prod[:, 0, 0:S], ALU.add
                                    ).then_inc(up_used.sem, 1)
                for m in range(8):
                    dve.wait_ge(tile_done.sem, tile_done.at(l, T_OUT + m + 1))
                    V.scalar_tensor_tensor(xT[:, m, :], bank[4 + m % 4][:, 0:S], 0.5, xT[:, m, :],
                                           ALU.mult, ALU.add).then_inc(out_used.sem, 1)
                norm(2, C_G2)

                taken = [0]
                with dve.Fori(0, TT) as tt:
                    dve.drain()
                    dve.sem_clear(route_chain)

                    def step(ins):
                        taken[0] += 1
                        ins.then_inc(route_chain, 1)
                        dve.wait_ge(route_chain, taken[0])

                    dve.wait_ge(score_copied.sem, tt * 4 + score_copied.at(l, 4))
                    step(V.tensor_copy(s_cur[:, :, :].rearrange("p a b -> p (a b)"),
                                       s_all[:, bass.ds(tt, 1), :].rearrange("p a b -> p (a b)")))
                    for m in range(2 * PH):
                        step(V.max(top_s[:, m, 0:8], s_cur[:, m, :]))
                        V.max_index(top_i[:, m, 0:8], top_s[:, m, 0:8], s_cur[:, m, :])
                        step(V.match_replace(s_rest[:, m, :], top_s[:, m, 0:8], s_cur[:, m, :], LOWEST))
                        step(V.max(top_s[:, m, 8:16], s_rest[:, m, :]))
                        V.max_index(top_i[:, m, 8:16], top_s[:, m, 8:16], s_rest[:, m, :])
                    sides = top_s[:, :, :].rearrange("p (h s) k -> p h s k", s=2)
                    wide = [P, PH, TOPK, TOPK]
                    step(V.tensor_tensor(cand[:, :, :, :], sides[:, :, 0, :].unsqueeze(3).to_broadcast(wide),
                                         sides[:, :, 1, :].unsqueeze(2).to_broadcast(wide), ALU.add))
                    for h in range(PH):
                        c = cand[:, h, :, :].rearrange("p a b -> p (a b)")
                        b0, b1 = best_s[:, h * TOPK:h * TOPK + 8], best_s[:, h * TOPK + 8:h * TOPK + 16]
                        step(V.max(b0, c))
                        V.max_index(best_i[:, h, 0:8], b0, c)
                        step(V.match_replace(cand_rest[:, h, :], b0, c, LOWEST))
                        step(V.max(b1, cand_rest[:, h, :]))
                        step(V.max_index(best_i[:, h, 8:16], b1, cand_rest[:, h, :]))
                    flat_i = best_i[:, :, :].rearrange("p h k -> p (h k)")
                    V.tensor_scalar(rank[:, 0, :], flat_i, 4, None, ALU.logical_shift_right)
                    step(V.tensor_scalar(rank[:, 1, :], flat_i, TOPK - 1, None, ALU.bitwise_and))
                    V.tensor_copy(rank_f[:, :, :], rank[:, :, :])
                    V.tensor_copy(best_all[:, bass.ds(tt, 1), :].rearrange("p a k -> p (a k)"), best_s[:, :])
                    step(V.tensor_copy(top_if[:, :, :, :].rearrange("p h s k -> p (h s) k"), top_i[:, :, :]))
                    for side in range(2):
                        shape3 = [P, PH * TOPK, TOPK]
                        step(V.tensor_tensor(pick[:, :, :], rank_f[:, side, :].unsqueeze(2).to_broadcast(shape3),
                                             iota_k[:, :].unsqueeze(1).to_broadcast(shape3), ALU.is_equal))
                        pick4 = pick[:, :, :].rearrange("p (h k) a -> p h k a", h=PH)
                        step(V.tensor_tensor(pick4, pick4,
                                             top_if[:, :, side, :].unsqueeze(2).to_broadcast(wide), ALU.mult))
                        step(V.tensor_reduce(slots[:, bass.ds(tt, 1), side, :].rearrange("p a k -> p (a k)"),
                                             pick[:, :, :], AX, ALU.add))
                best_v = best_all[:, :, :].rearrange("p t (h k) -> p (t h) k", k=TOPK)
                expd_v = expd[:, :, :].rearrange("p t (h k) -> p (t h) k", k=TOPK)
                shape = [P, TT * PH, TOPK]
                V.tensor_tensor(expd_v, best_v, best_v[:, :, 0:1].to_broadcast(shape), ALU.subtract
                                ).then_inc(best_ready.sem, 1)
                dve.wait_ge(expd_ready.sem, expd_ready.at(l, 1))
                den = top_if[:, :, :, :].rearrange("p a b c -> p (a b c)")
                link(V.tensor_reduce(den[:, 0:16], expd_v, AX, ALU.add))
                link(V.reciprocal(den[:, 16:32], den[:, 0:16]))
                for tt in range(TT):
                    ins = V.tensor_tensor(slots[:, tt, 2, :].rearrange("p (h k) -> p h k", k=TOPK),
                                          expd[:, tt, :].rearrange("p (h k) -> p h k", k=TOPK),
                                          den[:, 16 + 8 * tt:24 + 8 * tt].unsqueeze(2).to_broadcast([P, PH, TOPK]),
                                          ALU.mult)
                ins.then_inc(slots_ready.sem, 1)
                for tt in range(TT):
                    dve.wait_ge(slotT_done.sem, slotT_done.at(l, tt + 1))
                    ins = V.tensor_copy(slotT[:, :, tt * P:(tt + 1) * P],
                                        bank[2 + tt][:, 0:3 * P].rearrange("p (c t) -> p c t", c=3))
                ins.then_inc(route_done.sem, 1)

                for half in range(2):
                    keys = iota[:, half * HALF:(half + 1) * HALF]
                    with dve.Fori(0, HALF // RING) as i:
                        dve.drain()
                        dve.sem_clear(onehot_chain)
                        dve.wait_ge(gelu_done.sem, gelu_done.at(l, (half + 1) * HALF))
                        for s in range(RING):
                            def slot_row(c, n):
                                return slotT[:, c, bass.ds(i * (RING * TOK) + s * TOK, TOK)].unsqueeze(2
                                    ).to_broadcast([P, TOK, n])

                            V.tensor_tensor(onehot_i[:, :, :], iota[:, :].unsqueeze(1).to_broadcast([P, TOK, NK]),
                                            slot_row(0, NK), ALU.is_equal)
                            ins = V.tensor_tensor(onehot_j[:, :, :], keys.unsqueeze(1).to_broadcast([P, TOK, HALF]),
                                                  slot_row(1, HALF), ALU.is_equal)
                            ins.then_inc(onehot_chain, 1)
                            dve.wait_ge(onehot_chain, s + 1)
                            V.tensor_tensor(onehot_j[:, :, :], onehot_j[:, :, :], slot_row(2, HALF), ALU.mult
                                            ).then_inc(onehot_ready.sem, 1)
                            dve.wait_ge(g_done.sem, g_done.at(l, i * RING + (half * HALF + s + 1)))
                            w = experts[:, half * HALF:(half + 1) * HALF,
                                        bass.ds(i * (RING * TOK) + s * TOK, TOK)]
                            V.tensor_tensor(w, w, bank[2][:, 0:TOK * HALF].rearrange("p (t j) -> p j t", t=TOK),
                                            ALU.mult).then_inc(g_used.sem, 1)
                dve.wait_ge(acc_closed.sem, acc_closed.at(l, 1))
                for b in range(4):
                    ins = V.tensor_tensor(xT[:, 2 * b:2 * b + 2, :].rearrange("p a t -> p (a t)"), bank[4 + b][:, :],
                                          xT[:, 2 * b:2 * b + 2, :].rearrange("p a t -> p (a t)"), ALU.add)
                ins.then_inc(layer_open, 1)

        @block.tensor
        def _(pe):
            T = nc.tensor

            with pe.Fori(0, DEPTH) as l:
                def arrived(group, slot):
                    pe.wait_ge(ring_full[slot].sem, ring_full[slot].at(l, 16 * (group + 1)))

                def contract(out_, slot, rhs, n_k, k0=0):
                    for k in range(n_k):
                        ins = T.matmul(out_, ring[:, slot, (k0 + k) * P:(k0 + k + 1) * P], rhs[:, k, :],
                                       start=(k == 0), stop=(k == n_k - 1))
                    return ins

                def project(tile, m):
                    arrived(tile // RING, tile % RING)
                    if m >= 4:
                        pe.wait_ge(tile_copied.sem, tile_copied.at(l, m - 3))
                    contract(bank[m % 4][:, 0:S], tile % RING, hT, KT).then_inc(tile_done.sem, 1)

                def mean_square(n):
                    pe.wait_ge(sq_ready.sem, sq_ready.at(l, n))
                    for k in range(KT):
                        ins = T.matmul(bank[4][:, 0:S], mean_all, squares[:, k, :], start=(k == 0),
                                       stop=(k == KT - 1))
                    ins.then_inc(ms_done.sem, 1)
                    
                pe.wait_ge(consts_in, 48)
                pe.wait_ge(small_in.sem, small_in.at(l, small_in.per_layer))
                mean_square(1)
                T.matmul(bank[5][0:FFN, 0:S], w1[0:POS, :], pos[0:POS, :], start=True, stop=True
                         ).then_inc(ffn_done.sem, 1)
                pe.wait_ge(h_ready.sem, h_ready.at(l, 1))
                for m in range(8):
                    if m == 7:
                        pe.wait_ge(sin_done.sem, sin_done.at(l, 1))
                    project(T_QK + m, m)
                T.matmul(bank[5][0:FFN, 0:S], w2[0:FFN, :], h1[0:FFN, :], start=True, stop=True
                         ).then_inc(ffn_done.sem, 1)
                for n in range(4):
                    slot = (T_V + n) % RING
                    arrived((T_V + n) // RING, slot)
                    for tt in range(TT):
                        for k in range(2):
                            ins = T.matmul(bank[6 + tt][:, :], hT[:, 2 * n + k, tt * P:(tt + 1) * P],
                                           ring[:, slot, k * HW:(k + 1) * HW], start=(n == 0 and k == 0),
                                           stop=(n == 3 and k == 1))
                    ins.then_inc(tile_done.sem, 1)
                for n in range(4):
                    project(T_HY + n, 8 + n)
                pe.wait_ge(arg_ready.sem, arg_ready.at(l, 2))
                for n in range(4):
                    if n >= 2:
                        pe.wait_ge(qk_ready.sem, qk_ready.at(l, n - 1))
                    T.matmul(bank[4 + n % 2][:, :], mean_head, qk_sq[:, 2 * n:2 * n + 2, :].rearrange(
                        "p a t -> p (a t)"), start=True, stop=True).then_inc(ss_done.sem, 1)
                for n in range(4, 8):
                    project(T_HY + n, 8 + n)
                pe.wait_ge(sin_done.sem, sin_done.at(l, 2))
                pe.wait_ge(w3_ready.sem, w3_ready.at(l, 1))
                pe.wait_ge(qk_ready.sem, qk_ready.at(l, 4))
                pe.wait_ge(v_ready.sem, v_ready.at(l, 2))
                for n in range(4):
                    sd, tt = n // TT, n % TT
                    T.matmul(bank[4 + n][:, :], h2[0:FFN, tt * P:(tt + 1) * P], w3_sd[0:FFN, sd, :],
                             start=True, stop=True).then_inc(taps_done.sem, 1)
                for n in range(8, 12):
                    project(T_HY + n, 8 + n)
                pe.wait_ge(filters_ready.sem, filters_ready.at(l, 4))
                for n in range(4):
                    ri, f = n // TT, n % TT
                    for k in range(TT):
                        ins = T.matmul(bank[4 + n][:, :], dft[:, ri, k, f * P:(f + 1) * P], filters[:, ri, k, :],
                                       start=(k == 0), stop=(k == TT - 1))
                    ins.then_inc(spec_done.sem, 1)

                def head_scores(h):
                    r0, m = (h % 2) * HD, h // 2
                    if h >= 2:
                        pe.wait_ge(scores_ready.sem, scores_ready.at(l, h - 1))
                    for qt in range(TT):
                        ins = T.matmul(bank[4 + h % 2][:, qt * S:(qt + 1) * S],
                                       qk_n[r0:r0 + HD, m, qt * P:(qt + 1) * P], qk_n[r0:r0 + HD, 4 + m, :],
                                       start=True, stop=True)
                    ins.then_inc(scores_done.sem, 1)

                pe.wait_ge(spec_ready.sem, spec_ready.at(l, 4))
                head_scores(0)
                head_scores(1)
                for h in range(NH):
                    project(T_GATE + 2 * h, 20 + 2 * h)
                    pe.wait_ge(probs_ready.sem, probs_ready.at(l, h + 1))
                    if h:
                        pe.wait_ge(pT_ready.sem, pT_ready.at(l, h))
                    for qt in range(TT):
                        for kt in range(TT):
                            ins = T.transpose(bank[6][:, kt * S + qt * P:kt * S + (qt + 1) * P],
                                              probs[:, h % 2, qt, kt * P:(kt + 1) * P], identity)
                    ins.then_inc(pT_done.sem, 1)
                    project(T_GATE + 2 * h + 1, 20 + 2 * h + 1)
                    pe.wait_ge(pT_ready.sem, pT_ready.at(l, h + 1))
                    if h >= 2 and h % 2 == 0:
                        pe.wait_ge(attn_ready.sem, attn_ready.at(l, h // 2))
                    r0 = (h % 2) * HD
                    for kt in range(TT):
                        ins = T.matmul(bank[7][r0:r0 + HD, 0:S], v_tok[:, kt, h * HD:(h + 1) * HD],
                                       probs_T[:, h % 2, kt, :], start=(kt == 0), stop=(kt == TT - 1))
                    ins.then_inc(pv_done.sem, 1)
                    if h + 2 < NH:
                        head_scores(h + 2)
                pe.wait_ge(z_ready.sem, z_ready.at(l, 1))
                for tt in range(TT):
                    for ct in range(4):
                        ins = T.transpose(bank[4 + tt][:, ct * P:(ct + 1) * P], zT[:, ct, tt * P:(tt + 1) * P],
                                          identity)
                    ins.then_inc(zt_done.sem, 1)
                pe.wait_ge(zt_ready.sem, zt_ready.at(l, TT))
                pe.wait_ge(attn_ready.sem, attn_ready.at(l, NH // 2))
                for f in range(TT):
                    for ri in range(2):
                        b = (bank[6], bank[7])[ri] if f == 0 else (bank[4], bank[5])[ri]
                        for k in range(TT):
                            ins = T.matmul(b[:, :], dft[:, ri, k, f * P:(f + 1) * P], z_tok[:, k, :],
                                           start=(k == 0), stop=(k == TT - 1))
                    ins.then_inc(zf_done.sem, 1)
                pe.wait_ge(y_ready.sem, y_ready.at(l, TT))
                for ct in range(4):
                    for ri in range(2):
                        for f in range(TT):
                            ins = T.matmul(bank[6 + ct // 2][:, (ct % 2) * S:(ct % 2 + 1) * S],
                                           spec_y[:, ri, f, ct * P:(ct + 1) * P], dft[:, 2 + ri, f, :],
                                           start=(ri == 0 and f == 0), stop=(ri == 1 and f == TT - 1))
                    ins.then_inc(conv_done.sem, 1)
                pe.wait_ge(tile_copied.sem, tile_copied.at(l, 36))
                pe.wait_ge(hyena_ready.sem, hyena_ready.at(l, 4))
                for m in range(8):
                    arrived(T_UP // RING, m)
                    if m >= 4:
                        pe.wait_ge(up_used.sem, up_used.at(l, m - 3))
                    contract(bank[m % 4][:, 0:S], m, attn_T, 4)
                    contract(bank[m % 4][:, S:2 * S], m, hyena_T, 4, 4).then_inc(tile_done.sem, 1)
                pe.wait_ge(up_used.sem, up_used.at(l, 8))
                for m in range(8):
                    arrived(T_OUT // RING, m)
                    if m >= 4:
                        pe.wait_ge(out_used.sem, out_used.at(l, m - 3))
                    contract(bank[4 + m % 4][:, 0:S], m, merged, KT).then_inc(tile_done.sem, 1)
                mean_square(2)
                with pe.Fori(0, 2) as w:
                    pe.wait_ge(h_ready.sem, h_ready.at(l, 2))
                    for s in range(RING):
                        pe.wait_ge(ring_full[s].sem, ring_full[s].at(l, w * 16 + 16 * (T_WQ // RING + 1)))
                        pe.wait_ge(tile_copied.sem, tile_copied.at(l, w * RING + (36 + s - 3)))
                        contract(bank[s % 4][:, 0:S], s, hT, KT).then_inc(tile_done.sem, 1)
                pe.wait_ge(tile_copied.sem, tile_copied.at(l, 52))
                pe.wait_ge(subk_in.sem, subk_in.at(l, 16))
                for n in range(8):
                    tt, g = n // 4, n % 4
                    if n >= 4:
                        pe.wait_ge(score_copied.sem, score_copied.at(l, n - 3))
                    for c in range(4):
                        m = 4 * g + c
                        ins = T.matmul(bank[4 + g][:, c * P:(c + 1) * P], q2T[:, m, tt * P:(tt + 1) * P],
                                       subk[:, m, :], start=True, stop=True)
                    ins.then_inc(score_done.sem, 1)

                def u_tile(i, s, first):
                    pe.wait_ge(ring_full[s].sem, ring_full[s].at(l, i * 16 + 16 * ((T_U + first) // RING + 1)))
                    if first + s >= 2:
                        pe.wait_ge(gelu_done.sem, gelu_done.at(l, i * RING + (first + s - 1)))
                    contract(bank[s % 2][:, 0:S], s, hT, KT).then_inc(tile_done.sem, 1)

                def routing_weights(i, s, half):
                    pe.wait_ge(onehot_ready.sem, onehot_ready.at(l, i * RING + (half * HALF + s + 1)))
                    for t in range(TOK):
                        ins = T.matmul(bank[2][:, t * HALF:(t + 1) * HALF], onehot_i[:, t, :], onehot_j[:, t, :],
                                       start=True, stop=True)
                    ins.then_inc(g_done.sem, 1)

                def v_tile(i, s, first):
                    pe.wait_ge(ring_full[s].sem, ring_full[s].at(l, i * 16 + 16 * ((T_VT + first) // RING + 1)))
                    for ct in range(KT):
                        ins = T.matmul(bank[4 + ct // 2][:, (ct % 2) * S:(ct % 2 + 1) * S],
                                       ring[:, s, ct * P:(ct + 1) * P],
                                       experts[:, bass.ds(i * RING + (first + s), 1), :].rearrange(
                                           "p a t -> p (a t)"),
                                       start=False, stop=False, skip_group_check=True)
                    ins.then_inc(tile_done.sem, 1)

                with pe.Fori(0, HALF // RING) as i:
                    for s in range(RING):
                        pe.wait_ge(ring_full[s].sem, ring_full[s].at(l, i * 16 + 16 * (T_U // RING + 1)))
                        if s >= 2:
                            pe.wait_ge(gelu_done.sem, gelu_done.at(l, i * RING + (s - 1)))
                        contract(bank[s % 2][:, 0:S], s, hT, KT).then_inc(tile_done.sem, 1)
                    pe.wait_ge(gelu_done.sem, gelu_done.at(l, i * RING + RING))
                pe.wait_ge(slots_ready.sem, slots_ready.at(l, 1))
                for tt in range(TT):
                    for c in range(3):
                        ins = T.transpose(bank[2 + tt][:, c * P:(c + 1) * P], slots[:, tt, c, :], identity)
                    ins.then_inc(slotT_done.sem, 1)
                with pe.Fori(0, HALF // RING) as i:
                    for s in range(RING):
                        u_tile(i, s, HALF)
                        routing_weights(i, s, 0)
                for b in range(4):
                    T.matmul(bank[4 + b][:, :], zeros[:, 0:P], zeros[:, :], start=True, stop=False,
                             skip_group_check=True)
                with pe.Fori(0, HALF // RING) as i:
                    pe.wait_ge(g_used.sem, g_used.at(l, HALF))
                    for s in range(RING):
                        v_tile(i, s, 0)
                        routing_weights(i, s, 1)
                with pe.Fori(0, HALF // RING) as i:
                    pe.wait_ge(g_used.sem, g_used.at(l, 2 * HALF))
                    for s in range(RING):
                        v_tile(i, s, HALF)
                for b in range(4):
                    ins = T.matmul(bank[4 + b][:, :], zeros[:, 0:P], zeros[:, :], start=False, stop=True,
                                   skip_group_check=True)
                ins.then_inc(acc_closed.sem, 1)


def constants():
    f32 = np.float32
    t = np.linspace(0.0, 1.0, S, dtype=f32)[:, None]
    w = (2.0 * math.pi * np.arange(S, dtype=f32)[:, None] / S).astype(f32)
    f = np.linspace(1e-4, BANDS - 1, BANDS, dtype=f32)[None, :]
    pos = np.concatenate([t, np.cos(f * w), -np.sin(f * w)], axis=-1).astype(f32)
    lo, hi = math.log(1e-2) / 1.5, math.log(1e-2) / 0.3
    deltas = np.linspace(lo, hi, HW, dtype=f32)
    decay = np.exp(-t * np.abs(deltas)[None, :]).astype(f32)
    theta = np.outer(np.arange(S), np.arange(S) + 0.5) * (2.0 * math.pi / (2 * S))
    ahead = np.stack([np.cos(theta), -np.sin(theta)])
    back = np.stack([np.cos(theta.T), -np.sin(theta.T)]) / S
    dft = np.concatenate([ahead, back]).astype(f32).reshape(4, TT, P, S).transpose(2, 0, 1, 3)
    c = np.arange(GRID_W)
    c0 = np.clip(c - KW // 2, 0, GRID_W - KW)
    inside = (c[None, :] >= c0[:, None]) & (c[None, :] < c0[:, None] + KW)
    mask = np.tile(np.where(inside, 0.0, -1e30).astype(f32), (2, ROWS))
    head = np.kron(np.eye(P // HD), np.full((HD, HD), 1.0 / HD))
    mats = np.stack([np.eye(P), np.full((P, P), 1.0 / D), head], axis=1).astype(f32)
    iota = np.tile(np.arange(P, dtype=f32), (P, 1))
    return {
        "pos_in": np.ascontiguousarray(pos.T), "dft_in": np.ascontiguousarray(dft),
        "decay_in": np.ascontiguousarray(decay.reshape(TT, P, HW).transpose(1, 0, 2)),
        "mask_in": mask, "mats_in": mats, "iota_in": iota,
    }


def by_tiles(w):
    k, m = w.shape
    return w.reshape(k // P, P, m // P, P).transpose(2, 1, 0, 3).reshape(m // P, P, k)


def layer_stream(l, w_in, w_up_na, w_up_hy, w_out, peer_wq, peer_u, peer_v):
    na, hy = NH * HD, HW
    v = w_in[l][:, 2 * na:3 * na].reshape(4, 2, P, na).transpose(0, 2, 1, 3).reshape(4, P, D)
    up = np.concatenate([w_up_na[l], w_up_hy[l]], axis=0)
    ut = peer_u[l].reshape(NK, NK, KT, P).transpose(1, 3, 2, 0).reshape(NK, P, D)
    vt = peer_v[l].reshape(NK, NK, D).transpose(1, 0, 2)
    return [by_tiles(w_in[l][:, 0:2 * na]), v, by_tiles(w_in[l][:, 3 * na:3 * na + 3 * hy]),
            by_tiles(w_in[l][:, 3 * na + 3 * hy:]), by_tiles(up), by_tiles(w_out[l]), by_tiles(peer_wq[l]),
            ut, vt]


def kernel(**inputs):
    import concourse.bacc as bacc
    from concourse.bass_utils import run_bass_kernel_spmd

    a = {k: np.asarray(v) for k, v in inputs.items()}
    tiles = []
    for l in range(DEPTH):
        tiles += layer_stream(l, *(a[n] for n in ("w_in", "w_up_na", "w_up_hy", "w_out", "peer_wq",
                                                  "peer_u", "peer_v")))

    def column(v):
        return v.reshape(DEPTH, -1, P).transpose(0, 2, 1)

    gate_b = a["gate_b"].reshape(DEPTH, 2 * D)
    taps = a["hy_conv_w"].reshape(DEPTH, 3, 12, P).transpose(0, 3, 2, 1).reshape(DEPTH, P, 36)
    cols = np.concatenate([
        column(a["norm1_g"]), column(a["norm2_g"]), column(gate_b),
        np.tile(a["na_q_g"], (1, 2))[:, :, None], np.tile(a["na_k_g"], (1, 2))[:, :, None],
        taps, column(a["hy_conv_b"])], axis=2)
    c = np.arange(GRID_W)
    dc = np.clip(c[None, :] - c[:, None] + KW - 1, 0, 2 * KW - 2)
    dr = np.arange(KR_MAX - ROWS, KR_MAX + ROWS - 1)
    rpb = a["na_rpb"][:, :, dr][:, :, :, dc].transpose(0, 3, 1, 2, 4)
    arrays = {
        "x_in": a["x"][0].T.reshape(KT, P, S).transpose(1, 0, 2),
        "stream": np.concatenate(tiles, axis=0),
        "subkeys": a["peer_subkeys"].reshape(DEPTH, 2 * PH, NK, P).transpose(0, 3, 1, 2),
        "cols": cols.transpose(1, 0, 2),
        "ffn_cols": np.stack([a["hy_b1"], a["hy_freq"], a["hy_b2"]], axis=2),
        "w1_in": a["hy_w1"], "w2_in": a["hy_w2"], "w3_in": a["hy_w3"].reshape(DEPTH, FFN, 2, HW),
        "skip_in": a["hy_bias"], "rpb_in": rpb, **constants(),
    }
    arrays = {k: np.ascontiguousarray(v) for k, v in arrays.items()}
    nc = bacc.Bacc("TRN2", target_bir_lowering=False, num_devices=1)
    aps = {k: nc.dram_tensor(k, v.shape, mybir.dt.from_np(v.dtype), kind="ExternalInput").ap()
           for k, v in arrays.items()}
    out = nc.dram_tensor("out", (P, KT, S), F32, kind="ExternalOutput").ap()
    encoder_kernel(nc, out=out, **aps)
    r = run_bass_kernel_spmd(nc, [arrays], core_ids=[0])
    y = r.results[0]["out"]
    return np.ascontiguousarray(y.transpose(1, 0, 2).reshape(D, S).T[None])
```

```python
import math
from contextlib import ExitStack

import numpy as np

import concourse.bass as bass
from concourse import mybir
from concourse.alu_op_type import AluOpType as ALU

P = 128
D = 1024
S = 256
DEPTH = 2
GRID_W = 64
ROWS = S // GRID_W
NH = 8
HD = 64
KR_MAX = 8
KW = 16
HW = 512
BANDS = 16
POS = 1 + 2 * BANDS
FFN = 64
PH = 8
NK = 128
TOPK = 16
EPS = 1e-6

KT = D // P
TT = S // P
RING = 4
HT = D // 2
T_QK, T_V, T_HY, T_GATE = 0, 8, 12, 24
T_UP, T_OUT, T_WQ, T_U = 40, 48, 56, 72
T_VT = T_U + NK
TILES = T_VT + NK
GROUPS = TILES // RING
AHEAD = 2
HALF = NK // 2
TOK = S // HALF

C_G1, C_G2, C_GB, C_QG, C_KG, C_CW, C_CB = 0, 8, 16, 32, 33, 34, 70
N_COLS = 82

F32 = mybir.dt.float32
BF16 = mybir.dt.bfloat16
F32R = mybir.dt.float32r
U32 = mybir.dt.uint32
ACT = mybir.ActivationFunctionType
AX = mybir.AxisListType.X
POOL_TILES = T_U + HALF + AHEAD
LOWEST = -3.0e38
MAGIC = 1.5 * 2.0 ** 23
TWO_PI_HI = 6.28125
TWO_PI_LO = 2.0 * math.pi - TWO_PI_HI
PI_BELOW = 3.1415925


class Signal:

    def __init__(self, sem, per_layer):
        self.sem, self.per_layer = sem, per_layer

    def at(self, layer, count):
        return layer * self.per_layer + count


def encoder_kernel(nc, x_in, stream, subkeys, cols, ffn_cols, w1_in, w2_in, w3_in, skip_in, rpb_in,
                   pos_in, dft_in, decay_in, mask_in, mats_in, iota_in, out):
    ctx = ExitStack()
    with ctx:
        def sb(name, shape, dt=F32):
            return ctx.enter_context(nc.sbuf_tensor(name, shape, dt))

        def sem(name):
            return ctx.enter_context(nc.semaphore(name))

        def sig(name, per_layer):
            return Signal(sem(name), per_layer)

        arena = sb("arena", [P, NK * S])
        ring = sb("ring", [P, RING, D])
        xT = sb("xT", [P, KT, S])
        act_hi = sb("act_hi", [P, KT, S], F32R)
        act_lo = sb("act_lo", [P, KT, S], F32R)
        w_hi = sb("w_hi", [P, 2 * AHEAD, HT], F32R)
        w_lo = sb("w_lo", [P, 2 * AHEAD, HT], F32R)
        e_hi = sb("e_hi", [P, AHEAD, S], F32R)
        e_lo = sb("e_lo", [P, AHEAD, S], F32R)
        mats = sb("mats", [P, 3, P])
        iota = sb("iota", [P, P])
        iota_k = sb("iota_k", [P, TOPK])
        eps_col = sb("eps_col", [P, 1])
        iota_t = sb("iota_t", [P, NK, TOK], BF16)
        zeros = sb("zeros", [P, 512], BF16)
        all_cols = sb("all_cols", [P, DEPTH, N_COLS])
        col = sb("col", [P, N_COLS])
        half_gate_b = sb("half_gate_b", [P, 16])
        norm_tmp = sb("norm_tmp", [P, 3, S])
        soft = sb("soft", [P, 2, 3, TT])
        slotT = sb("slotT", [P, 5, S], BF16)
        w_rest = sb("w_rest", [P, P])
        onehot_i = sb("onehot_i", [P, 2, NK, TOK], BF16)
        onehot_j = sb("onehot_j", [P, 2, HALF, TOK], BF16)
        weighted_j = sb("weighted_j", [P, 2, 3, HALF, TOK], BF16)
        bank = [ctx.enter_context(nc.psum_tensor(f"bank{i}", [P, 512], F32)) for i in range(8)]

        identity, mean_all, mean_head = mats[:, 0, :], mats[:, 1, :], mats[:, 2, :]
        experts = arena[:, :].rearrange("p (j t) -> p j t", t=S)

        def part(kb, *dims, dt=F32):
            n = int(np.prod(dims))
            v = arena[:, int(kb * 256):int(kb * 256) + n]
            if dt != F32:
                v = v.bitcast(dt)
            names = "abcd"[:len(dims)]
            if len(dims) > 1:
                sizes = {c: d for c, d in zip(names[1:], dims[1:])}
                v = v.rearrange(f"p ({' '.join(names)}) -> p {' '.join(names)}", **sizes)
            return v

        squares = part(0, KT, S)
        hT = part(0, KT, S)
        spectrum = part(0, 2, TT, HW)
        merged = part(0, KT, S)
        qk_raw = part(8, 8, S)
        zT = part(8, 4, S)
        z_tok = part(12, TT, HW)
        qk_sq = part(16, 8, S)
        attn_T = part(16, 4, S)
        hyena_T = part(20, 4, S)
        qk_n = part(24, 8, S)
        v_tok = part(32, TT, HW)
        u_pad = part(36, 12, S + 2)
        prod = part(36, 2, HW)
        u = part(49, 12, S)
        gates = part(61, 16, S)
        h1, h2, arg, turns = part(61, S), part(62, S), part(63, S), part(64, S)
        w3 = part(65, 2, HW)
        w3_sd = part(69, 2, HW)
        w1 = part(73, FFN)
        w2 = part(73.25, FFN)
        ffn_col = part(73.5, 4)
        bias = part(77, NH, TT, S)
        scores = part(93, 2, TT, S)
        probs = part(97, 2, TT, S)
        qk_tmp = part(93, 3, 512)
        probs_T = part(101, 2, TT, S)
        dft = part(105, 4, TT, S)
        decay = part(113, TT, HW)
        mask = part(117, S)
        pos = part(118, S)
        filters = part(119, 2, TT, HW)
        spec_y = part(119, 2, TT, HW)
        q2T = part(24, 2 * PH, S)
        subk = part(40, 2 * PH, NK)
        s_all = part(64, TT, 2 * PH * NK)
        s_cur = part(80, 2 * PH, NK)
        s_rest = part(88, 2 * PH, NK)
        cand = part(96, PH, TOPK, TOPK)
        cand_rest = part(104, PH, TOPK * TOPK)
        pick = part(112, PH * TOPK, TOPK)
        top_s = part(120, 2 * PH, TOPK)
        top_i = part(121, 2 * PH, TOPK, dt=U32)
        top_if = part(122, PH, 2, TOPK)
        best_s = part(123, PH * TOPK)
        best_i = part(123.5, PH, TOPK, dt=U32)
        rank = part(124, 2, PH * TOPK, dt=U32)
        rank_f = part(125, 2, PH * TOPK)
        best_all = part(126, TT, PH * TOPK)
        expd = part(127, TT, PH * TOPK)
        slots = norm_tmp[:, :, :].rearrange("p a b -> p (a b)").rearrange("p (t c s) -> p t c s", t=TT, c=3)

        consts_in = sem("consts_in")
        x_loaded = sem("x_loaded")
        small_in = sig("small_in", 16 * (9 + ROWS))
        subk_in = sig("subk_in", 16)
        ring_full = [sig(f"ring_full{s}", 16 * GROUPS) for s in range(RING)]
        hi_ready = sig("hi_ready", 2 * TILES)
        lo_ready = [sig(f"lo_ready{half}", TILES) for half in range(2)]
        tile_done = sig("tile_done", TILES)
        e_hi_ready = sig("e_hi_ready", NK)
        e_lo_ready = sig("e_lo_ready", NK)
        layer_open = sem("layer_open")
        layer_chain = sem("layer_chain")
        setup_done = sig("setup_done", 1)
        sq_ready = sig("sq_ready", 2)
        ms_done = sig("ms_done", 2)
        y0_ready = sig("y0_ready", 2)
        h_ready = sig("h_ready", KT)
        ffn_done = sig("ffn_done", 2)
        arg_ready = sig("arg_ready", 2)
        sin_done = sig("sin_done", 2)
        tile_copied = sig("tile_copied", 52)
        v_ready = sig("v_ready", 2)
        ss_done = sig("ss_done", 4)
        qk_y0 = sig("qk_y0", 4)
        qk_ready = sig("qk_ready", 4)
        w3_ready = sig("w3_ready", 1)
        taps_done = sig("taps_done", 4)
        filters_ready = sig("filters_ready", 4)
        spec_done = sig("spec_done", 4)
        spec_ready = sig("spec_ready", 4)
        scores_done = sig("scores_done", NH)
        scores_ready = sig("scores_ready", NH)
        exp_done = sig("exp_done", NH)
        probs_ready = sig("probs_ready", NH)
        pT_done = sig("pT_done", NH)
        pT_ready = sig("pT_ready", NH)
        pv_done = sig("pv_done", NH)
        attn_ready = sig("attn_ready", NH // 2)
        z_ready = sig("z_ready", 1)
        zt_done = sig("zt_done", TT)
        zt_ready = sig("zt_ready", TT)
        zf_done = sig("zf_done", TT)
        y_ready = sig("y_ready", TT)
        attn_split = sig("attn_split", 1)
        merged_split = sig("merged_split", KT // 2)
        conv_done = sig("conv_done", 4)
        hyena_ready = sig("hyena_ready", 4)
        up_used = sig("up_used", 8)
        out_used = sig("out_used", 8)
        score_done = sig("score_done", 8)
        score_copied = sig("score_copied", 8)
        gelu_done = sig("gelu_done", NK)
        best_ready = sig("best_ready", 1)
        expd_ready = sig("expd_ready", 1)
        slots_ready = sig("slots_ready", 1)
        slotT_done = sig("slotT_done", TT)
        route_done = sig("route_done", 1)
        onehot_ready = sig("onehot_ready", 2 * HALF)
        g_done = sig("g_done", 2 * HALF)
        g_used = sig("g_used", 2 * HALF)
        acc_closed = sig("acc_closed", 1)
        act_chain = sem("act_chain")
        dve_chain = sem("dve_chain")
        route_chain = sem("route_chain")
        onehot_chain = sem("onehot_chain")
        stored = sem("stored")

        block = ctx.enter_context(nc.Block())

        @block.sync
        def _(sp):
            def load(n, slot):
                sp.dma_start(ring[:, slot, :], stream[bass.ds(n, 1), :, :].rearrange("a p n -> (a p) n")
                             ).then_inc(ring_full[slot].sem, 16)

            for slot in range(RING):
                load(slot, slot)
            with sp.Fori(1, DEPTH * GROUPS) as turn:
                for slot in range(RING):
                    for half in range(2):
                        sp.wait_ge(lo_ready[half].sem, turn * RING + (slot + 1 - RING))
                    load(turn * RING + slot, slot)
            sp.wait_ge(layer_open, DEPTH + 1)
            sp.dma_start(out, xT[:, :, :]).then_inc(stored, 16)
            sp.wait_ge(stored, 16)

        def low_parts(eng, l, i, tile, halves=(0, 1)):
            for half in halves:
                eng.wait_ge(hi_ready.sem, hi_ready.at(l, i * (2 * RING) + (2 * tile + half + 1)))
                part_ = 2 * (tile % AHEAD) + half
                eng.tensor_tensor(w_lo[:, part_, :], ring[:, tile % RING, half * HT:(half + 1) * HT],
                                  w_hi[:, part_, :].bitcast(F32), ALU.subtract).then_inc(lo_ready[half].sem, 1)

        @block.gpsimd
        def _(pool):
            with pool.Fori(0, DEPTH) as l:
                turns_ = POOL_TILES // RING
                with pool.Fori(0, turns_) as i:
                    pool.wait_ge(layer_chain, l + 1)
                    for s in range(RING):
                        low_parts(pool, l, i, s)
                for s in range(POOL_TILES % RING):
                    low_parts(pool, l, 0, turns_ * RING + s)
                with pool.Fori(0, HALF // RING - 1) as i:
                    for s in range(RING):
                        low_parts(pool, l, i, POOL_TILES + s, [1])
                for n in range(POOL_TILES + HALF - RING, T_VT + AHEAD):
                    low_parts(pool, l, 0, n, [1])

                def expert_low(i, n):
                    pool.wait_ge(e_hi_ready.sem, e_hi_ready.at(l, i * RING + (n + 1)))
                    pool.tensor_tensor(e_lo[:, n % AHEAD, :], experts[:, bass.ds(i * RING + n, 1), :].rearrange(
                        "p a t -> p (a t)"), e_hi[:, n % AHEAD, :].bitcast(F32), ALU.subtract
                        ).then_inc(e_lo_ready.sem, 1)

                for first in (0, HALF):
                    for n in range(AHEAD):
                        expert_low(0, first + n)
                    with pool.Fori(0, HALF // RING - 1) as i:
                        for s in range(RING):
                            expert_low(i, first + s + AHEAD)
                            low_parts(pool, l, i, T_VT + first + s + AHEAD, [1])
                    for n in range(first + HALF - RING, first + HALF):
                        if n + AHEAD < first + HALF:
                            expert_low(0, n + AHEAD)
                        if T_VT + n + AHEAD < TILES:
                            low_parts(pool, l, 0, T_VT + n + AHEAD, [1])

        @block.scalar
        def _(act):
            steps = [0]

            def high_parts(l, i, tile):
                slot = ring_full[tile % RING]
                act.wait_ge(slot.sem, slot.at(l, i * 16 + 16 * (tile // RING + 1)))
                if tile >= AHEAD:
                    act.wait_ge(tile_done.sem, tile_done.at(l, i * RING + (tile + 1 - AHEAD)))
                for half in range(2):
                    nc.scalar.activation(w_hi[:, 2 * (tile % AHEAD) + half, :],
                                         ring[:, tile % RING, half * HT:(half + 1) * HT], ACT.Copy
                                         ).then_inc(hi_ready.sem, 1)

            act.dma_start(xT[:, :, :], x_in).then_inc(x_loaded, 16)
            act.dma_start(mats[:, :, :], mats_in).then_inc(consts_in, 16)
            act.dma_start(iota[:, :], iota_in).then_inc(consts_in, 16)
            act.dma_start(all_cols[:, :, :], cols).then_inc(consts_in, 16)

            with act.Fori(0, DEPTH) as l:
                n_split = [0]

                def split_next():
                    n = n_split[0]
                    n_split[0] += 1
                    high_parts(l, 0, n)

                act.drain()
                act.sem_clear(act_chain)

                def link(ins):
                    steps[0] += 1
                    ins.then_inc(act_chain, 1)
                    act.wait_ge(act_chain, steps[0])

                def rsqrt_guess(tmp, src, done):
                    link(nc.scalar.activation(tmp[:, 1, :], src, ACT.Ln, bias=eps_col[:, :]))
                    nc.scalar.activation(tmp[:, 0, :], tmp[:, 1, :], ACT.Exp, scale=-0.5).then_inc(done, 1)

                def tile_wait(tile):
                    assert n_split[0] == tile + AHEAD
                    split_next()

                def copy_tile(tile, m, dst):
                    tile_wait(tile)
                    nc.scalar.activation(dst, bank[m % 4][:, 0:S], ACT.Copy).then_inc(tile_copied.sem, 1)

                def norm(n):
                    nc.scalar.activation(squares[:, :, :], xT[:, :, :], ACT.Square).then_inc(sq_ready.sem, 1)
                    act.wait_ge(ms_done.sem, ms_done.at(l, n))
                    rsqrt_guess(norm_tmp, bank[4][:, 0:S], y0_ready.sem)

                for _ in range(AHEAD):
                    split_next()
                act.wait_ge(layer_open, l + 1)

                def load(dst, src):
                    act.dma_start(dst, src).then_inc(small_in.sem, 16)

                at = bass.ds(l, 1)
                load(w1[0:POS, :], w1_in[at].rearrange("a p n -> (a p) n"))
                load(w2[0:FFN, :], w2_in[at].rearrange("a p n -> (a p) n"))
                load(w3[0:FFN, :, :], w3_in[at].rearrange("a p b n -> (a p) b n"))
                load(ffn_col[0:FFN, 0:3], ffn_cols[at].rearrange("a p n -> (a p) n"))
                load(part(74, HW)[0:1, :], skip_in[at, :])
                load(pos[0:POS, :], pos_in)
                load(decay[:, :, :], decay_in)
                load(mask, mask_in)
                load(dft[:, :, :, :], dft_in)
                for r in range(ROWS):
                    qt, p0 = r // 2, (r % 2) * GRID_W
                    load(bias[p0:p0 + GRID_W, :, qt, :].rearrange("c h (k n) -> c h k n", k=ROWS),
                         rpb_in[at, :, :, ROWS - 1 - r:2 * ROWS - 1 - r, :].rearrange("a c h k n -> (a c) h k n"))
                act.wait_ge(setup_done.sem, setup_done.at(l, 1))
                norm(1)
                for m in range(8):
                    tile_wait(T_QK + m)
                    nc.scalar.activation(qk_raw[:, m, :], bank[m % 4][:, 0:S], ACT.Copy)
                    nc.scalar.activation(qk_sq[:, m, :], bank[m % 4][:, 0:S], ACT.Square
                                         ).then_inc(tile_copied.sem, 1)
                act.wait_ge(arg_ready.sem, arg_ready.at(l, 1))
                nc.scalar.activation(h1[0:FFN, :], arg[0:FFN, :], ACT.Sin).then_inc(sin_done.sem, 1)
                for n in range(4):
                    tile_wait(T_V + n)
                for tt in range(TT):
                    nc.scalar.activation(v_tok[:, tt, :], bank[6 + tt][:, :], ACT.Copy).then_inc(v_ready.sem, 1)
                for n in range(4):
                    copy_tile(T_HY + n, 8 + n, u_pad[:, n, 1:S + 1])
                act.wait_ge(arg_ready.sem, arg_ready.at(l, 2))
                nc.scalar.activation(h2[0:FFN, :], arg[0:FFN, :], ACT.Sin).then_inc(sin_done.sem, 1)
                for n in range(4):
                    act.wait_ge(ss_done.sem, ss_done.at(l, n + 1))
                    if n:
                        act.wait_ge(qk_ready.sem, qk_ready.at(l, n))
                    rsqrt_guess(qk_tmp, bank[4 + n % 2][:, :], qk_y0.sem)
                for n in range(4, 12):
                    copy_tile(T_HY + n, 8 + n, u_pad[:, n, 1:S + 1])
                for n in range(4):
                    act.wait_ge(spec_done.sem, spec_done.at(l, n + 1))
                    nc.scalar.activation(spectrum[:, n // TT, n % TT, :], bank[4 + n][:, :], ACT.Copy
                                         ).then_inc(spec_ready.sem, 1)

                def gate(m):
                    tile_wait(T_GATE + m)
                    nc.scalar.activation(gates[:, m, :], bank[m % 4][:, 0:S], ACT.Tanh, scale=0.5,
                                         bias=half_gate_b[:, m:m + 1]).then_inc(tile_copied.sem, 1)

                def head_exp(h):
                    act.wait_ge(scores_ready.sem, scores_ready.at(l, h + 1))
                    for qt in range(TT):
                        last = nc.scalar.activation(probs[:, h % 2, qt, :], scores[:, h % 2, qt, :], ACT.Exp,
                                                    bias=soft[:, h % 2, 0, qt:qt + 1],
                                                    accum_out=soft[:, h % 2, 1, qt:qt + 1])
                        if qt == 0:
                            link(last)
                    last.then_inc(exp_done.sem, 1)

                head_exp(0)
                head_exp(1)
                for h in range(NH):
                    gate(2 * h)
                    act.wait_ge(pT_done.sem, pT_done.at(l, h + 1))
                    nc.scalar.activation(probs_T[:, h % 2, :, :], bank[6][:, :].rearrange(
                        "p (k q) -> p k q", k=TT), ACT.Copy).then_inc(pT_ready.sem, 1)
                    gate(2 * h + 1)
                    if h + 2 < NH:
                        head_exp(h + 2)
                for tt in range(TT):
                    act.wait_ge(zt_done.sem, zt_done.at(l, tt + 1))
                    nc.scalar.activation(z_tok[:, tt, :], bank[4 + tt][:, :], ACT.Copy).then_inc(zt_ready.sem, 1)
                for n in range(T_UP, T_WQ):
                    tile_wait(n)
                act.wait_ge(hyena_ready.sem, hyena_ready.at(l, 4))
                act.dma_start(subk[:, :, :], subkeys[at].rearrange("a p m n -> (a p) m n")
                              ).then_inc(subk_in.sem, 16)
                act.wait_ge(out_used.sem, out_used.at(l, 8))
                norm(2)
                with act.Fori(0, (T_U - T_WQ) // RING) as w:
                    for s in range(RING):
                        high_parts(l, w, T_WQ + s + AHEAD)
                        nc.scalar.activation(q2T[:, bass.ds(w * RING + s, 1), :].rearrange("p a t -> p (a t)"),
                                             bank[s % 4][:, 0:S], ACT.Copy).then_inc(tile_copied.sem, 1)
                for n in range(8):
                    tt, g = n // 4, n % 4
                    act.wait_ge(score_done.sem, score_done.at(l, n + 1))
                    nc.scalar.activation(s_all[:, tt, g * 512:(g + 1) * 512], bank[4 + g][:, :], ACT.Copy
                                         ).then_inc(score_copied.sem, 1)

                def gelus(first, count):
                    with act.Fori(0, count // RING) as i:
                        for s in range(RING):
                            high_parts(l, i, T_U + first + s + AHEAD)
                            nc.scalar.activation(experts[:, bass.ds(i * RING + (first + s), 1), :].rearrange(
                                "p a t -> p (a t)"), bank[s % 2][:, 0:S], ACT.Gelu_apprx_tanh
                                ).then_inc(gelu_done.sem, 1)

                def load_gelu():
                    nc.scalar.activation(w_rest[:, 0:1], eps_col[:, :], ACT.Gelu_apprx_tanh)

                load_gelu()
                gelus(0, 48)
                act.wait_ge(best_ready.sem, best_ready.at(l, 1))
                nc.scalar.activation(expd[:, :, :], expd[:, :, :], ACT.Exp).then_inc(expd_ready.sem, 1)
                load_gelu()
                gelus(48, 16)
                act.wait_ge(route_done.sem, route_done.at(l, 1))
                gelus(64, 64)

                def expert_high(i, n):
                    nc.scalar.activation(e_hi[:, n % AHEAD, :], experts[:, bass.ds(i * RING + n, 1), :].rearrange(
                        "p a t -> p (a t)"), ACT.Copy).then_inc(e_hi_ready.sem, 1)

                for half in range(2):
                    first = half * HALF
                    act.wait_ge(g_used.sem, g_used.at(l, first + HALF))
                    for n in range(AHEAD):
                        nc.scalar.activation(e_hi[:, n % AHEAD, :], experts[:, first + n, :], ACT.Copy
                                             ).then_inc(e_hi_ready.sem, 1)
                    with act.Fori(0, HALF // RING - 1) as i:
                        for s in range(RING):
                            act.wait_ge(tile_done.sem, tile_done.at(l, i * RING + (T_VT + first + s + 1)))
                            expert_high(i, first + s + AHEAD)
                            high_parts(l, i, T_VT + first + s + AHEAD)
                    for n in range(first + HALF - RING, first + HALF):
                        act.wait_ge(tile_done.sem, tile_done.at(l, T_VT + n + 1))
                        if n + AHEAD < first + HALF:
                            expert_high(0, n + AHEAD)
                        if T_VT + n + AHEAD < TILES:
                            high_parts(l, 0, T_VT + n + AHEAD)

        @block.vector
        def _(dve):
            count = [0]
            V = nc.vector
            V.memset(zeros[:, :], 0.0)
            V.memset(eps_col[:, :], EPS)
            dve.wait_ge(consts_in, 48)
            V.tensor_copy(iota_k[:, :], iota[:, 0:TOPK])
            V.tensor_copy(iota_t[:, :, :], iota[:, :].unsqueeze(2).to_broadcast([P, NK, TOK]))
            dve.wait_ge(x_loaded, 16)
            V.drain().then_inc(layer_open, 1)
            V.drain().then_inc(layer_chain, 1)

            with dve.Fori(0, DEPTH) as l:
                dve.drain()
                dve.sem_clear(dve_chain)

                def link(ins):
                    count[0] += 1
                    ins.then_inc(dve_chain, 1)
                    dve.wait_ge(dve_chain, count[0])

                def refine(tmp, src):
                    y0, t, y = tmp[:, 0, :], tmp[:, 1, :], tmp[:, 2, :]
                    link(V.tensor_tensor(t, y0, y0, ALU.mult))
                    link(V.scalar_tensor_tensor(t, src, EPS, t, ALU.add, ALU.mult))
                    link(V.tensor_scalar(t, t, -0.5, 1.5, ALU.mult, ALU.add))
                    link(V.tensor_tensor(y, y0, t, ALU.mult))

                def norm(n, gain):
                    dve.wait_ge(y0_ready.sem, y0_ready.at(l, n))
                    refine(norm_tmp, bank[4][:, 0:S])
                    for k in range(KT):
                        ins = V.scalar_tensor_tensor(hT[:, k, :], xT[:, k, :], col[:, gain + k:gain + k + 1],
                                                     norm_tmp[:, 2, :], ALU.mult, ALU.mult)
                        if k % 2:
                            link(ins)
                            two_parts(hT[:, k - 1:k + 1, :], k - 1, 2).then_inc(h_ready.sem, 1)

                def two_parts(src, k, n):
                    link(V.tensor_copy(act_hi[:, k:k + n, :], src))
                    return V.tensor_tensor(act_lo[:, k:k + n, :], src, act_hi[:, k:k + n, :].bitcast(F32),
                                           ALU.subtract)

                def sine_argument(n, b):
                    f = slice(0, FFN)
                    dve.wait_ge(ffn_done.sem, ffn_done.at(l, n))
                    link(V.tensor_scalar(arg[f, :], bank[5][f, 0:S], ffn_col[f, b:b + 1], ffn_col[f, 1:2],
                                         ALU.add, ALU.mult))
                    link(V.tensor_scalar(turns[f, :], arg[f, :], 1.0 / (2.0 * math.pi), MAGIC, ALU.mult, ALU.add))
                    link(V.tensor_scalar(turns[f, :], turns[f, :], MAGIC, None, ALU.subtract))
                    link(V.scalar_tensor_tensor(arg[f, :], turns[f, :], -TWO_PI_HI, arg[f, :], ALU.mult, ALU.add))
                    link(V.scalar_tensor_tensor(arg[f, :], turns[f, :], -TWO_PI_LO, arg[f, :], ALU.mult, ALU.add))
                    V.tensor_scalar(arg[f, :], arg[f, :], PI_BELOW, -PI_BELOW, ALU.min, ALU.max
                                    ).then_inc(arg_ready.sem, 1)

                V.tensor_copy(col[:, :], all_cols[:, bass.ds(l, 1), :].rearrange("p a n -> p (a n)"))
                V.tensor_scalar(half_gate_b[:, :], all_cols[:, bass.ds(l, 1), C_GB:C_GB + 16].rearrange(
                    "p a n -> p (a n)"), 0.5, None, ALU.mult)
                V.memset(u_pad[:, :, 0:1], 0.0)
                V.memset(u_pad[:, :, S + 1:S + 2], 0.0).then_inc(setup_done.sem, 1)
                norm(1, C_G1)
                dve.wait_ge(small_in.sem, small_in.at(l, small_in.per_layer))
                f = slice(0, FFN)
                V.tensor_tensor(w3_sd[f, 0, :], w3[f, 0, :], w3[f, 1, :], ALU.add)
                V.tensor_tensor(w3_sd[f, 1, :], w3[f, 0, :], w3[f, 1, :], ALU.subtract
                                ).then_inc(w3_ready.sem, 1)
                sine_argument(1, 0)
                dve.wait_ge(sin_done.sem, sin_done.at(l, 1))
                sine_argument(2, 2)

                for h in range(NH):
                    V.tensor_tensor(bias[:, h, :, :], bias[:, h, :, :],
                                    mask.unsqueeze(1).to_broadcast([P, TT, S]), ALU.add)

                for n in range(4):
                    dve.wait_ge(qk_y0.sem, qk_y0.at(l, n + 1))
                    refine(qk_tmp, bank[4 + n % 2][:, :])
                    gain = C_QG if n < 2 else C_KG
                    V.scalar_tensor_tensor(qk_n[:, 2 * n:2 * n + 2, :].rearrange("p a t -> p (a t)"),
                                           qk_raw[:, 2 * n:2 * n + 2, :].rearrange("p a t -> p (a t)"),
                                           col[:, gain:gain + 1], qk_tmp[:, 2, :], ALU.mult, ALU.mult
                                           ).then_inc(qk_ready.sem, 1)
                for n in range(4):
                    sd, tt = n // TT, n % TT
                    dve.wait_ge(taps_done.sem, taps_done.at(l, n + 1))
                    ins = V.tensor_tensor(filters[:, sd, tt, :], bank[4 + n][:, :], decay[:, tt, :], ALU.mult)
                    if n == 0:
                        link(ins)
                        ins = V.tensor_tensor(filters[0:1, 0, 0, :], filters[0:1, 0, 0, :],
                                              part(74, HW)[0:1, :], ALU.add)
                    ins.then_inc(filters_ready.sem, 1)

                def conv(n):
                    if n % 4 == 0:
                        dve.wait_ge(tile_copied.sem, tile_copied.at(l, 8 + n + 4))
                    w = C_CW + 3 * n
                    link(V.tensor_scalar(u[:, n, :], u_pad[:, n, 1:S + 1], col[:, w + 1:w + 2],
                                         col[:, C_CB + n:C_CB + n + 1], ALU.mult, ALU.add))
                    link(V.scalar_tensor_tensor(u[:, n, :], u_pad[:, n, 0:S], col[:, w:w + 1], u[:, n, :],
                                                ALU.mult, ALU.add))
                    link(V.scalar_tensor_tensor(u[:, n, :], u_pad[:, n, 2:S + 2], col[:, w + 2:w + 3], u[:, n, :],
                                                ALU.mult, ALU.add))

                def head_scores(h):
                    dve.wait_ge(scores_done.sem, scores_done.at(l, h + 1))
                    link(V.scalar_tensor_tensor(scores[:, h % 2, :, :].rearrange("p a t -> p (a t)"),
                                                bank[4 + h % 2][:, :], HD ** -0.5,
                                                bias[:, h, :, :].rearrange("p a t -> p (a t)"),
                                                ALU.mult, ALU.add))
                    V.tensor_reduce(soft[:, h % 2, 0, :], scores[:, h % 2, :, :], AX, ALU.max, negate=True
                                    ).then_inc(scores_ready.sem, 1)

                head_scores(0)
                head_scores(1)
                tiles = list(range(12))
                for h in range(NH):
                    dve.wait_ge(exp_done.sem, exp_done.at(l, h + 1))
                    link(V.reciprocal(soft[:, h % 2, 2, :], soft[:, h % 2, 1, :]))
                    for qt in range(TT):
                        ins = V.tensor_scalar(probs[:, h % 2, qt, :], probs[:, h % 2, qt, :],
                                              soft[:, h % 2, 2, qt:qt + 1], None, ALU.mult)
                        if qt == 0:
                            link(ins)
                    ins.then_inc(probs_ready.sem, 1)
                    for _ in range(2 - h % 2):
                        conv(tiles.pop(0))
                    if h + 2 < NH:
                        head_scores(h + 2)
                    if h % 2:
                        dve.wait_ge(pv_done.sem, pv_done.at(l, h + 1))
                        V.tensor_copy(attn_T[:, h // 2, :], bank[7][:, 0:S]).then_inc(attn_ready.sem, 1)
                V.tensor_tensor(zT[:, :, :], u[:, 4:8, :], u[:, 8:12, :], ALU.mult).then_inc(z_ready.sem, 1)
                dve.wait_ge(tile_done.sem, tile_done.at(l, T_UP))
                dve.wait_ge(attn_ready.sem, attn_ready.at(l, NH // 2))
                two_parts(attn_T[:, :, :], 0, 4).then_inc(attn_split.sem, 1)
                for f in range(TT):
                    re, im = (bank[6], bank[7]) if f == 0 else (bank[4], bank[5])
                    dve.wait_ge(zf_done.sem, zf_done.at(l, f + 1))
                    if f:
                        dve.wait_ge(y_ready.sem, y_ready.at(l, f))
                    V.tensor_tensor(prod[:, 0, :], re[:, :], spectrum[:, 0, f, :], ALU.mult)
                    link(V.tensor_tensor(prod[:, 1, :], im[:, :], spectrum[:, 1, f, :], ALU.mult))
                    link(V.tensor_tensor(spec_y[:, 0, f, :], prod[:, 0, :], prod[:, 1, :], ALU.subtract))
                    V.tensor_tensor(prod[:, 0, :], re[:, :], spectrum[:, 1, f, :], ALU.mult)
                    link(V.tensor_tensor(prod[:, 1, :], im[:, :], spectrum[:, 0, f, :], ALU.mult))
                    V.tensor_tensor(spec_y[:, 1, f, :], prod[:, 0, :], prod[:, 1, :], ALU.add
                                    ).then_inc(y_ready.sem, 1)
                for ct in range(4):
                    dve.wait_ge(conv_done.sem, conv_done.at(l, 2 * (ct // 2) + 2))
                    link(V.tensor_tensor(hyena_T[:, ct, :], bank[6 + ct // 2][:, (ct % 2) * S:(ct % 2 + 1) * S],
                                         u[:, ct, :], ALU.mult))
                    two_parts(hyena_T[:, ct:ct + 1, :], 4 + ct, 1).then_inc(hyena_ready.sem, 1)
                for m in range(8):
                    dve.wait_ge(tile_done.sem, tile_done.at(l, T_UP + m + 1))
                    b = bank[m % 4]
                    link(V.scalar_tensor_tensor(merged[:, m, :], gates[:, m, :], 1.0, b[:, 0:S], ALU.add, ALU.mult))
                    link(V.scalar_tensor_tensor(prod[:, 0, 0:S], gates[:, 8 + m, :], 1.0, b[:, S:2 * S],
                                                ALU.add, ALU.mult))
                    V.tensor_tensor(merged[:, m, :], merged[:, m, :], prod[:, 0, 0:S], ALU.add
                                    ).then_inc(up_used.sem, 1)
                dve.wait_ge(up_used.sem, up_used.at(l, 8))
                for k in range(0, KT, 2):
                    two_parts(merged[:, k:k + 2, :], k, 2).then_inc(merged_split.sem, 1)
                for m in range(8):
                    dve.wait_ge(tile_done.sem, tile_done.at(l, T_OUT + m + 1))
                    V.scalar_tensor_tensor(xT[:, m, :], bank[4 + m % 4][:, 0:S], 0.5, xT[:, m, :],
                                           ALU.mult, ALU.add).then_inc(out_used.sem, 1)
                norm(2, C_G2)

                taken = [0]
                with dve.Fori(0, TT) as tt:
                    dve.drain()
                    dve.sem_clear(route_chain)

                    def step(ins):
                        taken[0] += 1
                        ins.then_inc(route_chain, 1)
                        dve.wait_ge(route_chain, taken[0])

                    dve.wait_ge(score_copied.sem, tt * 4 + score_copied.at(l, 4))
                    step(V.tensor_copy(s_cur[:, :, :].rearrange("p a b -> p (a b)"),
                                       s_all[:, bass.ds(tt, 1), :].rearrange("p a b -> p (a b)")))
                    for m in range(2 * PH):
                        step(V.max(top_s[:, m, 0:8], s_cur[:, m, :]))
                        V.max_index(top_i[:, m, 0:8], top_s[:, m, 0:8], s_cur[:, m, :])
                        step(V.match_replace(s_rest[:, m, :], top_s[:, m, 0:8], s_cur[:, m, :], LOWEST))
                        step(V.max(top_s[:, m, 8:16], s_rest[:, m, :]))
                        V.max_index(top_i[:, m, 8:16], top_s[:, m, 8:16], s_rest[:, m, :])
                    sides = top_s[:, :, :].rearrange("p (h s) k -> p h s k", s=2)
                    wide = [P, PH, TOPK, TOPK]
                    step(V.tensor_tensor(cand[:, :, :, :], sides[:, :, 0, :].unsqueeze(3).to_broadcast(wide),
                                         sides[:, :, 1, :].unsqueeze(2).to_broadcast(wide), ALU.add))
                    for h in range(PH):
                        c = cand[:, h, :, :].rearrange("p a b -> p (a b)")
                        b0, b1 = best_s[:, h * TOPK:h * TOPK + 8], best_s[:, h * TOPK + 8:h * TOPK + 16]
                        step(V.max(b0, c))
                        V.max_index(best_i[:, h, 0:8], b0, c)
                        step(V.match_replace(cand_rest[:, h, :], b0, c, LOWEST))
                        step(V.max(b1, cand_rest[:, h, :]))
                        step(V.max_index(best_i[:, h, 8:16], b1, cand_rest[:, h, :]))
                    flat_i = best_i[:, :, :].rearrange("p h k -> p (h k)")
                    V.tensor_scalar(rank[:, 0, :], flat_i, 4, None, ALU.logical_shift_right)
                    step(V.tensor_scalar(rank[:, 1, :], flat_i, TOPK - 1, None, ALU.bitwise_and))
                    V.tensor_copy(rank_f[:, :, :], rank[:, :, :])
                    V.tensor_copy(best_all[:, bass.ds(tt, 1), :].rearrange("p a k -> p (a k)"), best_s[:, :])
                    step(V.tensor_copy(top_if[:, :, :, :].rearrange("p h s k -> p (h s) k"), top_i[:, :, :]))
                    for side in range(2):
                        shape3 = [P, PH * TOPK, TOPK]
                        step(V.tensor_tensor(pick[:, :, :], rank_f[:, side, :].unsqueeze(2).to_broadcast(shape3),
                                             iota_k[:, :].unsqueeze(1).to_broadcast(shape3), ALU.is_equal))
                        pick4 = pick[:, :, :].rearrange("p (h k) a -> p h k a", h=PH)
                        step(V.tensor_tensor(pick4, pick4,
                                             top_if[:, :, side, :].unsqueeze(2).to_broadcast(wide), ALU.mult))
                        step(V.tensor_reduce(slots[:, bass.ds(tt, 1), side, :].rearrange("p a k -> p (a k)"),
                                             pick[:, :, :], AX, ALU.add))
                best_v = best_all[:, :, :].rearrange("p t (h k) -> p (t h) k", k=TOPK)
                expd_v = expd[:, :, :].rearrange("p t (h k) -> p (t h) k", k=TOPK)
                shape = [P, TT * PH, TOPK]
                V.tensor_tensor(expd_v, best_v, best_v[:, :, 0:1].to_broadcast(shape), ALU.subtract
                                ).then_inc(best_ready.sem, 1)
                dve.wait_ge(expd_ready.sem, expd_ready.at(l, 1))
                den = top_if[:, :, :, :].rearrange("p a b c -> p (a b c)")
                link(V.tensor_reduce(den[:, 0:16], expd_v, AX, ALU.add))
                link(V.reciprocal(den[:, 16:32], den[:, 0:16]))
                for tt in range(TT):
                    ins = V.tensor_tensor(slots[:, tt, 2, :].rearrange("p (h k) -> p h k", k=TOPK),
                                          expd[:, tt, :].rearrange("p (h k) -> p h k", k=TOPK),
                                          den[:, 16 + 8 * tt:24 + 8 * tt].unsqueeze(2).to_broadcast([P, PH, TOPK]),
                                          ALU.mult)
                ins.then_inc(slots_ready.sem, 1)
                for tt in range(TT):
                    dve.wait_ge(slotT_done.sem, slotT_done.at(l, tt + 1))
                    cols_ = slice(tt * P, (tt + 1) * P)
                    src = bank[2 + tt][:, 0:3 * P].rearrange("p (c t) -> p c t", c=3)
                    link(V.tensor_copy(slotT[:, 0:3, cols_], src))
                    link(V.tensor_tensor(w_rest[:, :], src[:, 2, :], slotT[:, 2, cols_], ALU.subtract))
                    link(V.tensor_copy(slotT[:, 3, cols_], w_rest[:, :]))
                    link(V.tensor_tensor(w_rest[:, :], w_rest[:, :], slotT[:, 3, cols_], ALU.subtract))
                    ins = V.tensor_copy(slotT[:, 4, cols_], w_rest[:, :])
                    if tt == 0:
                        link(ins)
                ins.then_inc(route_done.sem, 1)

                def one_hots(half, i, n):
                    tokens = bass.ds(i * (RING * TOK) + n * TOK, TOK)

                    def over_keys(c, n_keys):
                        return slotT[:, c, tokens].unsqueeze(1).to_broadcast([P, n_keys, TOK])

                    V.tensor_tensor(onehot_j[:, n % 2, :, :], iota_t[:, half * HALF:(half + 1) * HALF, :],
                                    over_keys(1, HALF), ALU.is_equal).then_inc(onehot_chain, 1)
                    V.tensor_tensor(onehot_i[:, n % 2, :, :], iota_t[:, :, :], over_keys(0, NK), ALU.is_equal)
                    built[0] += 1
                    dve.wait_ge(onehot_chain, built[0])
                    V.tensor_tensor(weighted_j[:, n % 2, :, :, :],
                                    onehot_j[:, n % 2, :, :].unsqueeze(1).to_broadcast([P, 3, HALF, TOK]),
                                    slotT[:, 2:5, tokens].unsqueeze(2).to_broadcast([P, 3, HALF, TOK]),
                                    ALU.mult).then_inc(onehot_ready.sem, 1)

                def weight_experts(half, i, n):
                    if n % RING == 0:
                        dve.wait_ge(gelu_done.sem, gelu_done.at(l, (half + 1) * HALF))
                    dve.wait_ge(g_done.sem, g_done.at(l, i * RING + (half * HALF + n + 1)))
                    tokens = bass.ds(i * (RING * TOK) + n * TOK, TOK)
                    w = experts[:, half * HALF:(half + 1) * HALF, tokens]
                    V.tensor_tensor(w, w, bank[2 + n % 2][:, 0:TOK * HALF].rearrange("p (t j) -> p j t", t=TOK),
                                    ALU.mult).then_inc(g_used.sem, 1)

                built = [0]
                dve.drain()
                dve.sem_clear(onehot_chain)
                dve.wait_ge(lo_ready[0].sem, lo_ready[0].at(l, POOL_TILES))
                one_hots(0, 0, 0)
                one_hots(0, 0, 1)
                for half in range(2):
                    with dve.Fori(0, HALF // RING - 1) as i:
                        dve.drain()
                        dve.sem_clear(onehot_chain)
                        built = [0]
                        for s in range(RING):
                            low_parts(V, l, i, POOL_TILES + half * HALF + s, [0])
                            weight_experts(half, i, s)
                            one_hots(half, i, s + 2)
                    dve.drain()
                    dve.sem_clear(onehot_chain)
                    built = [0]
                    for n in range(HALF - RING, HALF):
                        low_parts(V, l, 0, POOL_TILES + half * HALF + n, [0])
                        weight_experts(half, 0, n)
                        if n + 2 < HALF:
                            one_hots(half, 0, n + 2)
                        elif half == 0:
                            one_hots(1, 0, n + 2 - HALF)
                with dve.Fori(0, HALF // RING - 1) as i:
                    for s in range(RING):
                        low_parts(V, l, i, T_VT + HALF + s + AHEAD, [0])
                for n in range(TILES - RING + AHEAD, TILES):
                    low_parts(V, l, 0, n, [0])
                V.drain().then_inc(layer_chain, 1)
                dve.wait_ge(acc_closed.sem, acc_closed.at(l, 1))
                for b in range(4):
                    ins = V.tensor_tensor(xT[:, 2 * b:2 * b + 2, :].rearrange("p a t -> p (a t)"), bank[4 + b][:, :],
                                          xT[:, 2 * b:2 * b + 2, :].rearrange("p a t -> p (a t)"), ALU.add)
                ins.then_inc(layer_open, 1)

        @block.tensor
        def _(pe):
            T = nc.tensor

            with pe.Fori(0, DEPTH) as l:
                def parts_ready(i, tile, half):
                    pe.wait_ge(lo_ready[half].sem, lo_ready[half].at(l, i * RING + (tile + 1)))

                def weights(part_, tile, k):
                    return part_[:, 2 * (tile % AHEAD) + k // 4, (k % 4) * P:(k % 4 + 1) * P]

                def contract(out_, i, tile, first=0, n_k=KT, wait=None):
                    for k in range(first, first + n_k):
                        if k % 4 == 0:
                            parts_ready(i, tile, k // 4)
                        if wait is not None:
                            wait(k)
                        T.matmul(out_, weights(w_hi, tile, k), act_hi[:, k, :], start=(k == first), stop=False)
                        T.matmul(out_, weights(w_hi, tile, k), act_lo[:, k, :], start=False, stop=False)
                        ins = T.matmul(out_, weights(w_lo, tile, k), act_hi[:, k, :], start=False,
                                       stop=(k == first + n_k - 1))
                    return ins

                def trunk_part(n):
                    def wait(k):
                        if k % 2 == 0:
                            pe.wait_ge(h_ready.sem, h_ready.at(l, (n - 1) * (KT // 2) + k // 2 + 1))
                    return wait

                def project(tile, m, wait=None):
                    if m >= 4:
                        pe.wait_ge(tile_copied.sem, tile_copied.at(l, m - 3))
                    contract(bank[m % 4][:, 0:S], 0, tile, wait=wait).then_inc(tile_done.sem, 1)

                def mean_square(n):
                    pe.wait_ge(sq_ready.sem, sq_ready.at(l, n))
                    for k in range(KT):
                        ins = T.matmul(bank[4][:, 0:S], mean_all, squares[:, k, :], start=(k == 0),
                                       stop=(k == KT - 1))
                    ins.then_inc(ms_done.sem, 1)
                    
                pe.wait_ge(consts_in, 48)
                mean_square(1)
                for m in range(8):
                    if m == 7:
                        pe.wait_ge(small_in.sem, small_in.at(l, small_in.per_layer))
                    project(T_QK + m, m, trunk_part(1) if m == 0 else None)
                T.matmul(bank[5][0:FFN, 0:S], w1[0:POS, :], pos[0:POS, :], start=True, stop=True
                         ).then_inc(ffn_done.sem, 1)
                for n in range(4):
                    for half in range(2):
                        parts_ready(0, T_V + n, half)
                        k, part_ = 2 * n + half, 2 * (n % AHEAD) + half
                        for tt in range(TT):
                            tokens = slice(tt * P, (tt + 1) * P)
                            T.matmul(bank[6 + tt][:, :], act_hi[:, k, tokens], w_hi[:, part_, :],
                                     start=(k == 0), stop=False)
                            T.matmul(bank[6 + tt][:, :], act_hi[:, k, tokens], w_lo[:, part_, :],
                                     start=False, stop=False)
                            ins = T.matmul(bank[6 + tt][:, :], act_lo[:, k, tokens], w_hi[:, part_, :],
                                           start=False, stop=(k == KT - 1))
                    ins.then_inc(tile_done.sem, 1)
                for n in range(4):
                    if n == 3:
                        pe.wait_ge(sin_done.sem, sin_done.at(l, 1))
                    project(T_HY + n, 8 + n)
                T.matmul(bank[5][0:FFN, 0:S], w2[0:FFN, :], h1[0:FFN, :], start=True, stop=True
                         ).then_inc(ffn_done.sem, 1)
                pe.wait_ge(arg_ready.sem, arg_ready.at(l, 2))
                for n in range(4):
                    if n >= 2:
                        pe.wait_ge(qk_ready.sem, qk_ready.at(l, n - 1))
                    T.matmul(bank[4 + n % 2][:, :], mean_head, qk_sq[:, 2 * n:2 * n + 2, :].rearrange(
                        "p a t -> p (a t)"), start=True, stop=True).then_inc(ss_done.sem, 1)
                for n in range(4, 8):
                    project(T_HY + n, 8 + n)
                pe.wait_ge(sin_done.sem, sin_done.at(l, 2))
                pe.wait_ge(w3_ready.sem, w3_ready.at(l, 1))
                pe.wait_ge(qk_ready.sem, qk_ready.at(l, 4))
                pe.wait_ge(v_ready.sem, v_ready.at(l, 2))
                for n in range(4):
                    sd, tt = n // TT, n % TT
                    T.matmul(bank[4 + n][:, :], h2[0:FFN, tt * P:(tt + 1) * P], w3_sd[0:FFN, sd, :],
                             start=True, stop=True).then_inc(taps_done.sem, 1)
                for n in range(8, 12):
                    project(T_HY + n, 8 + n)
                pe.wait_ge(filters_ready.sem, filters_ready.at(l, 4))
                for n in range(4):
                    ri, f = n // TT, n % TT
                    for k in range(TT):
                        ins = T.matmul(bank[4 + n][:, :], dft[:, ri, k, f * P:(f + 1) * P], filters[:, ri, k, :],
                                       start=(k == 0), stop=(k == TT - 1))
                    ins.then_inc(spec_done.sem, 1)

                def head_scores(h):
                    r0, m = (h % 2) * HD, h // 2
                    if h >= 2:
                        pe.wait_ge(scores_ready.sem, scores_ready.at(l, h - 1))
                    for qt in range(TT):
                        ins = T.matmul(bank[4 + h % 2][:, qt * S:(qt + 1) * S],
                                       qk_n[r0:r0 + HD, m, qt * P:(qt + 1) * P], qk_n[r0:r0 + HD, 4 + m, :],
                                       start=True, stop=True)
                    ins.then_inc(scores_done.sem, 1)

                pe.wait_ge(spec_ready.sem, spec_ready.at(l, 4))
                head_scores(0)
                head_scores(1)
                for h in range(NH):
                    project(T_GATE + 2 * h, 20 + 2 * h)
                    pe.wait_ge(probs_ready.sem, probs_ready.at(l, h + 1))
                    if h:
                        pe.wait_ge(pT_ready.sem, pT_ready.at(l, h))
                    for qt in range(TT):
                        for kt in range(TT):
                            ins = T.transpose(bank[6][:, kt * S + qt * P:kt * S + (qt + 1) * P],
                                              probs[:, h % 2, qt, kt * P:(kt + 1) * P], identity)
                    ins.then_inc(pT_done.sem, 1)
                    project(T_GATE + 2 * h + 1, 20 + 2 * h + 1)
                    pe.wait_ge(pT_ready.sem, pT_ready.at(l, h + 1))
                    if h >= 2 and h % 2 == 0:
                        pe.wait_ge(attn_ready.sem, attn_ready.at(l, h // 2))
                    r0 = (h % 2) * HD
                    for kt in range(TT):
                        ins = T.matmul(bank[7][r0:r0 + HD, 0:S], v_tok[:, kt, h * HD:(h + 1) * HD],
                                       probs_T[:, h % 2, kt, :], start=(kt == 0), stop=(kt == TT - 1))
                    ins.then_inc(pv_done.sem, 1)
                    if h + 2 < NH:
                        head_scores(h + 2)
                pe.wait_ge(z_ready.sem, z_ready.at(l, 1))
                for tt in range(TT):
                    for ct in range(4):
                        ins = T.transpose(bank[4 + tt][:, ct * P:(ct + 1) * P], zT[:, ct, tt * P:(tt + 1) * P],
                                          identity)
                    ins.then_inc(zt_done.sem, 1)
                pe.wait_ge(zt_ready.sem, zt_ready.at(l, TT))
                pe.wait_ge(attn_ready.sem, attn_ready.at(l, NH // 2))
                for f in range(TT):
                    for ri in range(2):
                        b = (bank[6], bank[7])[ri] if f == 0 else (bank[4], bank[5])[ri]
                        for k in range(TT):
                            ins = T.matmul(b[:, :], dft[:, ri, k, f * P:(f + 1) * P], z_tok[:, k, :],
                                           start=(k == 0), stop=(k == TT - 1))
                    ins.then_inc(zf_done.sem, 1)
                pe.wait_ge(y_ready.sem, y_ready.at(l, TT))
                for ct in range(4):
                    for ri in range(2):
                        for f in range(TT):
                            ins = T.matmul(bank[6 + ct // 2][:, (ct % 2) * S:(ct % 2 + 1) * S],
                                           spec_y[:, ri, f, ct * P:(ct + 1) * P], dft[:, 2 + ri, f, :],
                                           start=(ri == 0 and f == 0), stop=(ri == 1 and f == TT - 1))
                    ins.then_inc(conv_done.sem, 1)
                pe.wait_ge(tile_copied.sem, tile_copied.at(l, 36))
                pe.wait_ge(attn_split.sem, attn_split.at(l, 1))

                def hyena_part(k):
                    pe.wait_ge(hyena_ready.sem, hyena_ready.at(l, k - 3))

                for m in range(8):
                    if m >= 4:
                        pe.wait_ge(up_used.sem, up_used.at(l, m - 3))
                    contract(bank[m % 4][:, 0:S], 0, T_UP + m, 0, 4)
                    contract(bank[m % 4][:, S:2 * S], 0, T_UP + m, 4, 4,
                             hyena_part if m == 0 else None).then_inc(tile_done.sem, 1)

                def merged_part(k):
                    if k % 2 == 0:
                        pe.wait_ge(merged_split.sem, merged_split.at(l, k // 2 + 1))

                for m in range(8):
                    if m >= 4:
                        pe.wait_ge(out_used.sem, out_used.at(l, m - 3))
                    contract(bank[4 + m % 4][:, 0:S], 0, T_OUT + m, wait=merged_part if m == 0 else None
                             ).then_inc(tile_done.sem, 1)
                mean_square(2)
                for s in range(RING):
                    pe.wait_ge(tile_copied.sem, tile_copied.at(l, 36))
                    contract(bank[s % 4][:, 0:S], 0, T_WQ + s, wait=trunk_part(2) if s == 0 else None
                             ).then_inc(tile_done.sem, 1)
                with pe.Fori(1, (T_U - T_WQ) // RING) as w:
                    for s in range(RING):
                        pe.wait_ge(tile_copied.sem, tile_copied.at(l, w * RING + (36 + s - 3)))
                        contract(bank[s % 4][:, 0:S], w, T_WQ + s).then_inc(tile_done.sem, 1)
                pe.wait_ge(tile_copied.sem, tile_copied.at(l, 52))
                pe.wait_ge(subk_in.sem, subk_in.at(l, 16))
                for n in range(8):
                    tt, g = n // 4, n % 4
                    if n >= 4:
                        pe.wait_ge(score_copied.sem, score_copied.at(l, n - 3))
                    for c in range(4):
                        m = 4 * g + c
                        ins = T.matmul(bank[4 + g][:, c * P:(c + 1) * P], q2T[:, m, tt * P:(tt + 1) * P],
                                       subk[:, m, :], start=True, stop=True)
                    ins.then_inc(score_done.sem, 1)

                def u_tile(i, s, first):
                    if first + s >= 2:
                        pe.wait_ge(gelu_done.sem, gelu_done.at(l, i * RING + (first + s - 1)))
                    contract(bank[s % 2][:, 0:S], i, T_U + first + s).then_inc(tile_done.sem, 1)

                def routing_weights(i, s, half):
                    pe.wait_ge(onehot_ready.sem, onehot_ready.at(l, i * RING + (half * HALF + s + 1)))
                    for t in range(TOK):
                        for c in range(3):
                            ins = T.matmul(bank[2 + s % 2][:, t * HALF:(t + 1) * HALF], onehot_i[:, s % 2, :, t],
                                           weighted_j[:, s % 2, c, :, t], start=(c == 0), stop=(c == 2))
                    ins.then_inc(g_done.sem, 1)

                def v_tile(i, s, first):
                    pe.wait_ge(e_lo_ready.sem, e_lo_ready.at(l, i * RING + (first + s + 1)))
                    tile = T_VT + first + s
                    for ct in range(KT):
                        if ct % 4 == 0:
                            parts_ready(i, tile, ct // 4)
                        for w_, e_ in ((w_hi, e_hi), (w_hi, e_lo), (w_lo, e_hi)):
                            ins = T.matmul(bank[4 + ct // 2][:, (ct % 2) * S:(ct % 2 + 1) * S], weights(w_, tile, ct),
                                           e_[:, s % AHEAD, :], start=False, stop=False, skip_group_check=True)
                    ins.then_inc(tile_done.sem, 1)

                for s in range(RING):
                    u_tile(0, s, 0)
                with pe.Fori(0, HALF // RING - 1) as i:
                    for s in range(RING):
                        u_tile(i, s, RING)
                pe.wait_ge(slots_ready.sem, slots_ready.at(l, 1))
                for tt in range(TT):
                    for c in range(3):
                        ins = T.transpose(bank[2 + tt][:, c * P:(c + 1) * P], slots[:, tt, c, :], identity)
                    ins.then_inc(slotT_done.sem, 1)
                with pe.Fori(0, HALF // RING) as i:
                    for s in range(RING):
                        routing_weights(i, s, 0)
                        u_tile(i, s, HALF)
                for b in range(4):
                    T.matmul(bank[4 + b][:, :], zeros[:, 0:P], zeros[:, :], start=True, stop=False,
                             skip_group_check=True)
                with pe.Fori(0, HALF // RING) as i:
                    for s in range(RING):
                        routing_weights(i, s, 1)
                        v_tile(i, s, 0)
                with pe.Fori(0, HALF // RING) as i:
                    for s in range(RING):
                        v_tile(i, s, HALF)
                for b in range(4):
                    ins = T.matmul(bank[4 + b][:, :], zeros[:, 0:P], zeros[:, :], start=False, stop=True,
                                   skip_group_check=True)
                ins.then_inc(acc_closed.sem, 1)


def constants():
    f32 = np.float32
    t = np.linspace(0.0, 1.0, S, dtype=f32)[:, None]
    w = (2.0 * math.pi * np.arange(S, dtype=f32)[:, None] / S).astype(f32)
    f = np.linspace(1e-4, BANDS - 1, BANDS, dtype=f32)[None, :]
    pos = np.concatenate([t, np.cos(f * w), -np.sin(f * w)], axis=-1).astype(f32)
    lo, hi = math.log(1e-2) / 1.5, math.log(1e-2) / 0.3
    deltas = np.linspace(lo, hi, HW, dtype=f32)
    decay = np.exp(-t * np.abs(deltas)[None, :]).astype(f32)
    theta = np.outer(np.arange(S), np.arange(S) + 0.5) * (2.0 * math.pi / (2 * S))
    ahead = np.stack([np.cos(theta), -np.sin(theta)])
    back = np.stack([np.cos(theta.T), -np.sin(theta.T)]) / S
    dft = np.concatenate([ahead, back]).astype(f32).reshape(4, TT, P, S).transpose(2, 0, 1, 3)
    c = np.arange(GRID_W)
    c0 = np.clip(c - KW // 2, 0, GRID_W - KW)
    inside = (c[None, :] >= c0[:, None]) & (c[None, :] < c0[:, None] + KW)
    mask = np.tile(np.where(inside, 0.0, -1e30).astype(f32), (2, ROWS))
    head = np.kron(np.eye(P // HD), np.full((HD, HD), 1.0 / HD))
    mats = np.stack([np.eye(P), np.full((P, P), 1.0 / D), head], axis=1).astype(f32)
    iota = np.tile(np.arange(P, dtype=f32), (P, 1))
    return {
        "pos_in": np.ascontiguousarray(pos.T), "dft_in": np.ascontiguousarray(dft),
        "decay_in": np.ascontiguousarray(decay.reshape(TT, P, HW).transpose(1, 0, 2)),
        "mask_in": mask, "mats_in": mats, "iota_in": iota,
    }


def by_tiles(w):
    k, m = w.shape
    return w.reshape(k // P, P, m // P, P).transpose(2, 1, 0, 3).reshape(m // P, P, k)


def layer_stream(l, w_in, w_up_na, w_up_hy, w_out, peer_wq, peer_u, peer_v):
    na, hy = NH * HD, HW
    v = w_in[l][:, 2 * na:3 * na].reshape(4, 2, P, na).transpose(0, 2, 1, 3).reshape(4, P, D)
    up = np.concatenate([w_up_na[l], w_up_hy[l]], axis=0)
    ut = peer_u[l].reshape(NK, NK, KT, P).transpose(1, 3, 2, 0).reshape(NK, P, D)
    vt = peer_v[l].reshape(NK, NK, D).transpose(1, 0, 2)
    return [by_tiles(w_in[l][:, 0:2 * na]), v, by_tiles(w_in[l][:, 3 * na:3 * na + 3 * hy]),
            by_tiles(w_in[l][:, 3 * na + 3 * hy:]), by_tiles(up), by_tiles(w_out[l]), by_tiles(peer_wq[l]),
            ut, vt]


def kernel(**inputs):
    import concourse.bacc as bacc
    from concourse.bass_utils import run_bass_kernel_spmd

    a = {k: np.asarray(v) for k, v in inputs.items()}
    tiles = []
    for l in range(DEPTH):
        tiles += layer_stream(l, *(a[n] for n in ("w_in", "w_up_na", "w_up_hy", "w_out", "peer_wq",
                                                  "peer_u", "peer_v")))

    def column(v):
        return v.reshape(DEPTH, -1, P).transpose(0, 2, 1)

    gate_b = a["gate_b"].reshape(DEPTH, 2 * D)
    taps = a["hy_conv_w"].reshape(DEPTH, 3, 12, P).transpose(0, 3, 2, 1).reshape(DEPTH, P, 36)
    cols = np.concatenate([
        column(a["norm1_g"]), column(a["norm2_g"]), column(gate_b),
        np.tile(a["na_q_g"], (1, 2))[:, :, None], np.tile(a["na_k_g"], (1, 2))[:, :, None],
        taps, column(a["hy_conv_b"])], axis=2)
    c = np.arange(GRID_W)
    dc = np.clip(c[None, :] - c[:, None] + KW - 1, 0, 2 * KW - 2)
    dr = np.arange(KR_MAX - ROWS, KR_MAX + ROWS - 1)
    rpb = a["na_rpb"][:, :, dr][:, :, :, dc].transpose(0, 3, 1, 2, 4)
    arrays = {
        "x_in": a["x"][0].T.reshape(KT, P, S).transpose(1, 0, 2),
        "stream": np.concatenate(tiles, axis=0),
        "subkeys": a["peer_subkeys"].reshape(DEPTH, 2 * PH, NK, P).transpose(0, 3, 1, 2),
        "cols": cols.transpose(1, 0, 2),
        "ffn_cols": np.stack([a["hy_b1"], a["hy_freq"], a["hy_b2"]], axis=2),
        "w1_in": a["hy_w1"], "w2_in": a["hy_w2"], "w3_in": a["hy_w3"].reshape(DEPTH, FFN, 2, HW),
        "skip_in": a["hy_bias"], "rpb_in": rpb, **constants(),
    }
    arrays = {k: np.ascontiguousarray(v) for k, v in arrays.items()}
    nc = bacc.Bacc("TRN2", target_bir_lowering=False, num_devices=1)
    aps = {k: nc.dram_tensor(k, v.shape, mybir.dt.from_np(v.dtype), kind="ExternalInput").ap()
           for k, v in arrays.items()}
    out = nc.dram_tensor("out", (P, KT, S), F32, kind="ExternalOutput").ap()
    encoder_kernel(nc, out=out, **aps)
    r = run_bass_kernel_spmd(nc, [arrays], core_ids=[0])
    y = r.results[0]["out"]
    return np.ascontiguousarray(y.transpose(1, 0, 2).reshape(D, S).T[None])
```

```python
import math
from contextlib import ExitStack

import numpy as np

import concourse.bass as bass
from concourse import mybir
from concourse.alu_op_type import AluOpType as ALU

P = 128
D = 1024
S = 256
DEPTH = 2
GRID_W = 64
ROWS = S // GRID_W
NH = 8
HD = 64
KR_MAX = 8
KW = 16
HW = 512
BANDS = 16
POS = 1 + 2 * BANDS
FFN = 64
PH = 8
NK = 128
TOPK = 16
EPS = 1e-6

KT = D // P
TT = S // P
RING = 4
HT = D // 2
T_QK, T_V, T_HY, T_GATE = 0, 8, 12, 24
T_UP, T_OUT, T_WQ, T_U = 40, 48, 56, 72
T_VT = T_U + NK
TILES = T_VT + NK
GROUPS = TILES // RING
AHEAD = 2
ROUTED = 52
HALF = NK // 2
TOK = S // HALF

C_G1, C_G2, C_GB, C_QG, C_KG, C_CW, C_CB = 0, 8, 16, 32, 33, 34, 70
N_COLS = 82

F32 = mybir.dt.float32
BF16 = mybir.dt.bfloat16
F32R = mybir.dt.float32r
U32 = mybir.dt.uint32
ACT = mybir.ActivationFunctionType
AX = mybir.AxisListType.X
POOL_TILES = T_U + HALF + AHEAD
LOWEST = -3.0e38
MAGIC = 1.5 * 2.0 ** 23
TWO_PI_HI = 6.28125
TWO_PI_LO = 2.0 * math.pi - TWO_PI_HI
PI_BELOW = 3.1415925


class Signal:

    def __init__(self, sem, per_layer):
        self.sem, self.per_layer = sem, per_layer

    def at(self, layer, count):
        return layer * self.per_layer + count


def encoder_kernel(nc, x_in, stream, subkeys, cols, ffn_cols, w1_in, w2_in, w3_in, skip_in, rpb_in,
                   pos_in, dft_in, decay_in, spread_in, mask_in, mats_in, iota_in, out):
    ctx = ExitStack()
    with ctx:
        def sb(name, shape, dt=F32):
            return ctx.enter_context(nc.sbuf_tensor(name, shape, dt))

        def sem(name):
            return ctx.enter_context(nc.semaphore(name))

        def sig(name, per_layer):
            return Signal(sem(name), per_layer)

        arena = sb("arena", [P, NK * S])
        ring = sb("ring", [P, RING, D])
        xT = sb("xT", [P, KT, S])
        act_hi = sb("act_hi", [P, KT, S], F32R)
        act_lo = sb("act_lo", [P, KT, S], F32R)
        w_hi = sb("w_hi", [P, 2 * AHEAD, HT], F32R)
        w_lo = sb("w_lo", [P, 2 * AHEAD, HT], F32R)
        e_hi = sb("e_hi", [P, AHEAD, S], F32R)
        e_lo = sb("e_lo", [P, AHEAD, S], F32R)
        mats = sb("mats", [P, 3, P])
        iota = sb("iota", [P, P])
        iota_k = sb("iota_k", [P, TOPK])
        eps_col = sb("eps_col", [P, 1])
        iota_t = sb("iota_t", [P, NK, TOK], BF16)
        zeros = sb("zeros", [P, 512], BF16)
        all_cols = sb("all_cols", [P, DEPTH, N_COLS])
        col = sb("col", [P, N_COLS])
        half_gate_b = sb("half_gate_b", [P, 16])
        norm_tmp = sb("norm_tmp", [P, 3, S])
        soft = sb("soft", [P, 2, 3, TT])
        slotT = sb("slotT", [P, 5, S], BF16)
        table_dummy = sb("table_dummy", [P, 1])
        w_rest = sb("w_rest", [P, P])
        onehot_i = sb("onehot_i", [P, 2, NK, TOK], BF16)
        onehot_j = sb("onehot_j", [P, 2, HALF, TOK], BF16)
        weighted_j = sb("weighted_j", [P, 2, 3, HALF, TOK], BF16)
        bank = [ctx.enter_context(nc.psum_tensor(f"bank{i}", [P, 512], F32)) for i in range(8)]

        identity, mean_all, by_head = mats[:, 0, :], mats[:, 1, :], mats[:, 2, :]
        experts = arena[:, :].rearrange("p (j t) -> p j t", t=S)

        def part(kb, *dims, dt=F32):
            n = int(np.prod(dims))
            v = arena[:, int(kb * 256):int(kb * 256) + n]
            if dt != F32:
                v = v.bitcast(dt)
            names = "abcd"[:len(dims)]
            if len(dims) > 1:
                sizes = {c: d for c, d in zip(names[1:], dims[1:])}
                v = v.rearrange(f"p ({' '.join(names)}) -> p {' '.join(names)}", **sizes)
            return v

        squares = part(0, KT, S)
        hT = part(0, KT, S)
        spectrum = part(0, 2, TT, HW)
        merged = part(24, KT, S)
        qk_raw = part(8, 8, S)
        zT = part(8, 4, S)
        z_tok = part(12, TT, HW)
        qk_sq = part(16, 8, S)
        attn_T = part(16, 4, S)
        hyena_T = part(20, 4, S)
        qk_n = part(24, 8, S)
        v_tok = part(32, TT, HW)
        u_pad = part(36, 12, S + 2)
        prod = part(36, 2, HW)
        u = part(49, 12, S)
        gates = part(61, 16, S)
        h1, h2, arg, turns = part(61, S), part(62, S), part(63, S), part(64, S)
        w3 = part(65, 2, HW)
        w3_sd = part(69, 2, HW)
        w1 = part(73, FFN)
        w2 = part(73.25, FFN)
        ffn_col = part(73.5, 4)
        bias = part(77, NH, TT, S)
        scores = part(93, 2, TT, S)
        probs = part(97, 2, TT, S)
        qk_tmp = part(93, 3, S)
        spread = part(97, KT, P)
        probs_T = part(101, 2, TT, S)
        dft = part(105, 4, TT, S)
        decay = part(113, TT, HW)
        skip = part(74, HW)
        mask = part(117, S)
        pos = part(118, S)
        filters = part(119, 2, TT, HW)
        spec_y = part(119, 2, TT, HW)
        q2T = part(24, 2 * PH, S)
        subk = part(40, 2 * PH, NK)
        s_all = part(64, TT, 2 * PH * NK)
        s_cur = part(80, 2 * PH, NK)
        s_rest = part(88, 2 * PH, NK)
        cand = part(96, PH, TOPK, TOPK)
        cand_rest = part(104, PH, TOPK * TOPK)
        pick = part(112, PH * TOPK, TOPK)
        top_s = part(120, 2 * PH, TOPK)
        top_i = part(121, 2 * PH, TOPK, dt=U32)
        top_if = part(122, PH, 2, TOPK)
        best_s = part(123, PH * TOPK)
        best_i = part(123.5, PH, TOPK, dt=U32)
        rank = part(124, 2, PH * TOPK, dt=U32)
        rank_f = part(125, 2, PH * TOPK)
        best_all = part(126, TT, PH * TOPK)
        expd = part(127, TT, PH * TOPK)
        slots = norm_tmp[:, :, :].rearrange("p a b -> p (a b)").rearrange("p (t c s) -> p t c s", t=TT, c=3)

        consts_in = sem("consts_in")
        mats_loaded = sem("mats_loaded")
        x_loaded = [sem(f"x_loaded{b}") for b in range(KT // 2)]
        net_in = sig("net_in", 16 * 8)
        tables_in = sig("tables_in", 16 * (2 + ROWS))
        subk_in = sig("subk_in", 16)
        ring_full = [sig(f"ring_full{s}", 16 * GROUPS) for s in range(RING)]
        hi_ready = sig("hi_ready", 2 * TILES)
        lo_ready = [sig(f"lo_ready{half}", TILES) for half in range(2)]
        tile_done = sig("tile_done", TILES)
        e_hi_ready = sig("e_hi_ready", NK)
        e_lo_ready = sig("e_lo_ready", NK)
        trunk_in = sig("trunk_in", KT // 2)
        layer_chain = sem("layer_chain")
        setup_done = sig("setup_done", 1)
        sq_ready = sig("sq_ready", KT)
        ms_done = sig("ms_done", 2)
        root_ready = sig("root_ready", 2)
        h_made = sig("h_made", KT)
        h_hi_ready = sig("h_hi_ready", KT)
        h_ready = sig("h_ready", KT)
        ffn_done = sig("ffn_done", 2)
        arg_ready = sig("arg_ready", 2)
        sin_done = sig("sin_done", 2)
        tile_copied = sig("tile_copied", 52)
        v_ready = sig("v_ready", 2)
        ss_done = sig("ss_done", 1)
        qk_root = sig("qk_root", 1)
        qk_scale_ready = sig("qk_scale_ready", 1)
        spread_done = sig("spread_done", 4)
        qk_ready = sig("qk_ready", 4)
        w3_ready = sig("w3_ready", 1)
        taps_done = sig("taps_done", 4)
        filters_ready = sig("filters_ready", 4)
        spec_done = sig("spec_done", 4)
        spec_ready = sig("spec_ready", 4)
        scores_done = sig("scores_done", NH)
        scores_ready = sig("scores_ready", NH)
        exp_done = sig("exp_done", NH)
        probs_ready = sig("probs_ready", NH)
        pT_done = sig("pT_done", NH)
        pT_ready = sig("pT_ready", NH)
        pv_done = sig("pv_done", NH)
        attn_ready = sig("attn_ready", NH // 2)
        z_ready = sig("z_ready", 1)
        zt_done = sig("zt_done", TT)
        zt_ready = sig("zt_ready", TT)
        zf_done = sig("zf_done", TT)
        y_ready = sig("y_ready", TT)
        attn_split = sig("attn_split", 2)
        merged_split = sig("merged_split", KT // 2)
        conv_done = sig("conv_done", 4)
        hyena_ready = sig("hyena_ready", 4)
        up_used = sig("up_used", 16)
        out_used = sig("out_used", 8)
        score_done = sig("score_done", 8)
        score_copied = sig("score_copied", 8)
        gelu_done = sig("gelu_done", NK)
        best_ready = sig("best_ready", 1)
        expd_ready = sig("expd_ready", 1)
        slots_ready = sig("slots_ready", 1)
        slotT_done = sig("slotT_done", TT)
        route_done = sig("route_done", 1)
        onehot_ready = sig("onehot_ready", 2 * HALF)
        g_done = sig("g_done", 2 * HALF)
        g_used = sig("g_used", 2 * HALF)
        act_chain = sem("act_chain")
        dve_chain = sem("dve_chain")
        route_chain = sem("route_chain")
        onehot_chain = sem("onehot_chain")
        stored = sem("stored")

        block = ctx.enter_context(nc.Block())

        @block.sync
        def _(sp):
            def load(n, slot):
                sp.dma_start(ring[:, slot, :], stream[bass.ds(n, 1), :, :].rearrange("a p n -> (a p) n")
                             ).then_inc(ring_full[slot].sem, 16)

            def refill(turn, slot):
                for half in range(2):
                    sp.wait_ge(lo_ready[half].sem, turn * RING + (slot + 1 - RING))
                load(turn * RING + slot, slot)

            def layer_loads(l):
                at = bass.ds(l, 1)

                def small(signal, dst, src):
                    sp.dma_start(dst, src).then_inc(signal.sem, 16)

                def offsets(r):
                    qt, p0 = r // 2, (r % 2) * GRID_W
                    small(tables_in, bias[p0:p0 + GRID_W, :, qt, :].rearrange("c h (k n) -> c h k n", k=ROWS),
                          rpb_in[at, :, :, ROWS - 1 - r:2 * ROWS - 1 - r, :].rearrange("a c h k n -> (a c) h k n"))

                sp.wait_ge(trunk_in.sem, trunk_in.at(l, 1))
                small(net_in, w1[0:POS, :], w1_in[at].rearrange("a p n -> (a p) n"))
                small(net_in, pos[0:POS, :], pos_in)
                small(net_in, ffn_col[0:FFN, 0:3], ffn_cols[at].rearrange("a p n -> (a p) n"))
                small(net_in, w2[0:FFN, :], w2_in[at].rearrange("a p n -> (a p) n"))
                small(net_in, w3[0:FFN, :, :], w3_in[at].rearrange("a p b n -> (a p) b n"))
                small(net_in, skip[0:1, :], skip_in[at, :])
                small(net_in, decay[:, :, :], decay_in)
                small(net_in, spread[0:2 * NH, :, :], spread_in)
                refill(l * GROUPS + 1, 0)
                small(tables_in, mask, mask_in)
                refill(l * GROUPS + 1, 1)
                small(tables_in, dft[:, :, :, :], dft_in)
                for slot in range(2, RING):
                    refill(l * GROUPS + 1, slot)
                for r in range(ROWS):
                    refill(l * GROUPS + 2, r % RING)
                    offsets(r)
                with sp.Fori(l * GROUPS + 3, (l + 1) * GROUPS) as turn:
                    for slot in range(RING):
                        refill(turn, slot)

            for b in range(KT // 2):
                two = slice(2 * b, 2 * b + 2)
                sp.dma_start(xT[:, two, :], x_in[:, two, :]).then_inc(x_loaded[b], 16)
            for slot in range(RING):
                load(slot, slot)
            with sp.Fori(0, DEPTH - 1) as l:
                layer_loads(l)
                for slot in range(RING):
                    refill((l + 1) * GROUPS, slot)
            layer_loads(DEPTH - 1)
            sp.wait_ge(trunk_in.sem, trunk_in.at(DEPTH, KT // 2))
            sp.dma_start(out, xT[:, :, :]).then_inc(stored, 16)
            sp.wait_ge(stored, 16)

        def low_parts(eng, l, i, tile, halves=(0, 1)):
            for half in halves:
                eng.wait_ge(hi_ready.sem, hi_ready.at(l, i * (2 * RING) + (2 * tile + half + 1)))
                part_ = 2 * (tile % AHEAD) + half
                eng.tensor_tensor(w_lo[:, part_, :], ring[:, tile % RING, half * HT:(half + 1) * HT],
                                  w_hi[:, part_, :].bitcast(F32), ALU.subtract).then_inc(lo_ready[half].sem, 1)

        @block.gpsimd
        def _(pool):
            with pool.Fori(0, DEPTH) as l:
                turns_ = POOL_TILES // RING
                with pool.Fori(0, turns_) as i:
                    pool.wait_ge(layer_chain, l + 1)
                    for s in range(RING):
                        low_parts(pool, l, i, s)
                for s in range(POOL_TILES % RING):
                    low_parts(pool, l, 0, turns_ * RING + s)
                with pool.Fori(0, HALF // RING - 1) as i:
                    for s in range(RING):
                        low_parts(pool, l, i, POOL_TILES + s, [1])
                def expert_low(i, n):
                    pool.wait_ge(e_hi_ready.sem, e_hi_ready.at(l, i * RING + (n + 1)))
                    pool.tensor_tensor(e_lo[:, n % AHEAD, :], experts[:, bass.ds(i * RING + n, 1), :].rearrange(
                        "p a t -> p (a t)"), e_hi[:, n % AHEAD, :].bitcast(F32), ALU.subtract
                        ).then_inc(e_lo_ready.sem, 1)

                for n in range(POOL_TILES + HALF - RING, T_VT + AHEAD):
                    if n == T_VT + AHEAD - 1:
                        expert_low(0, 0)
                    low_parts(pool, l, 0, n, [1])
                expert_low(0, 1)

                def v_low(i, n):
                    expert_low(i, n + AHEAD)
                    low_parts(pool, l, i, T_VT + n + AHEAD, [1])

                with pool.Fori(0, HALF // RING - 1) as i:
                    for s in range(RING):
                        v_low(i, s)
                for n in range(HALF - RING, HALF):
                    if n == HALF - AHEAD:
                        low_parts(pool, l, 0, T_VT + n + AHEAD, [1])
                        expert_low(0, n + AHEAD)
                    else:
                        v_low(0, n)
                with pool.Fori(0, HALF // RING - 1) as i:
                    for s in range(RING):
                        v_low(i, HALF + s)
                for n in range(NK - RING, NK - AHEAD):
                    v_low(0, n)

        @block.scalar
        def _(act):
            steps = [0]

            def high_parts(l, i, tile):
                slot = ring_full[tile % RING]
                act.wait_ge(slot.sem, slot.at(l, i * 16 + 16 * (tile // RING + 1)))
                if tile >= AHEAD:
                    act.wait_ge(tile_done.sem, tile_done.at(l, i * RING + (tile + 1 - AHEAD)))
                for half in range(2):
                    nc.scalar.activation(w_hi[:, 2 * (tile % AHEAD) + half, :],
                                         ring[:, tile % RING, half * HT:(half + 1) * HT], ACT.Copy
                                         ).then_inc(hi_ready.sem, 1)

            act.dma_start(mats[:, :, :], mats_in).then_inc(mats_loaded, 16)
            act.dma_start(all_cols[:, :, :], cols).then_inc(consts_in, 16)
            act.dma_start(iota[:, :], iota_in).then_inc(consts_in, 16)

            with act.Fori(0, DEPTH) as l:
                n_split = [0]

                def split_next():
                    n = n_split[0]
                    n_split[0] += 1
                    high_parts(l, 0, n)

                act.drain()
                act.sem_clear(act_chain)

                def link(ins):
                    steps[0] += 1
                    ins.then_inc(act_chain, 1)
                    act.wait_ge(act_chain, steps[0])

                def root(tmp, src, n, done):
                    nc.scalar.activation(tmp[0:n, 0, :], src, ACT.Sqrt, bias=eps_col[0:n, :]).then_inc(done, 1)

                def load_table(function):
                    nc.scalar.activation(table_dummy[:, :], eps_col[:, :], function)

                def tile_wait(tile):
                    assert n_split[0] == tile + AHEAD
                    split_next()

                def copy_tile(tile, m, dst):
                    tile_wait(tile)
                    nc.scalar.activation(dst, bank[m % 4][:, 0:S], ACT.Copy).then_inc(tile_copied.sem, 1)

                def square(n, b):
                    two = slice(2 * b, 2 * b + 2)
                    nc.scalar.activation(squares[:, two, :], xT[:, two, :], ACT.Square).then_inc(sq_ready.sem, 1)

                def norm_root(n):
                    load_table(ACT.Sqrt)
                    act.wait_ge(ms_done.sem, ms_done.at(l, n))
                    root(norm_tmp, bank[3][:, 0:S], P, root_ready.sem)

                def norm_high(n):
                    for b in range(KT // 2):
                        act.wait_ge(h_made.sem, h_made.at(l, (n - 1) * (KT // 2) + b + 1))
                        nc.scalar.activation(act_hi[:, 2 * b:2 * b + 2, :], hT[:, 2 * b:2 * b + 2, :], ACT.Copy
                                             ).then_inc(h_hi_ready.sem, 1)

                for b in range(KT // 2):
                    act.wait_ge(trunk_in.sem, trunk_in.at(l, b + 1))
                    square(1, b)
                split_next()
                act.wait_ge(setup_done.sem, setup_done.at(l, 1))
                norm_root(1)
                split_next()
                norm_high(1)
                for m in range(8):
                    tile_wait(T_QK + m)
                    nc.scalar.activation(qk_raw[:, m, :], bank[m % 4][:, 0:S], ACT.Copy)
                    nc.scalar.activation(qk_sq[:, m, :], bank[m % 4][:, 0:S], ACT.Square
                                         ).then_inc(tile_copied.sem, 1)
                def hyena_in(n):
                    copy_tile(T_HY + n, 8 + n, u_pad[:, n, 1:S + 1])

                def sine(n, dst):
                    act.wait_ge(arg_ready.sem, arg_ready.at(l, n))
                    nc.scalar.activation(dst[0:FFN, :], arg[0:FFN, :], ACT.Sin).then_inc(sin_done.sem, 1)

                tile_wait(T_V)
                act.wait_ge(ss_done.sem, ss_done.at(l, 1))
                root(qk_tmp, bank[4][0:2 * NH, 0:S], 2 * NH, qk_root.sem)
                tile_wait(T_V + 1)
                sine(1, h1)
                tile_wait(T_V + 2)
                tile_wait(T_V + 3)
                for tt in range(TT):
                    nc.scalar.activation(v_tok[:, tt, :], bank[6 + tt][:, :], ACT.Copy).then_inc(v_ready.sem, 1)
                sine(2, h2)
                for n in range(7):
                    hyena_in(n)
                for n in range(4):
                    act.wait_ge(spec_done.sem, spec_done.at(l, n + 1))
                    nc.scalar.activation(spectrum[:, n // TT, n % TT, :], bank[4 + n][:, :], ACT.Copy
                                         ).then_inc(spec_ready.sem, 1)
                for n in range(7, 12):
                    hyena_in(n)

                def gate(m):
                    tile_wait(T_GATE + m)
                    nc.scalar.activation(gates[:, m, :], bank[m % 4][:, 0:S], ACT.Tanh, scale=0.5,
                                         bias=half_gate_b[:, m:m + 1]).then_inc(tile_copied.sem, 1)

                def head_exp(h):
                    act.wait_ge(scores_ready.sem, scores_ready.at(l, h + 1))
                    for qt in range(TT):
                        last = nc.scalar.activation(probs[:, h % 2, qt, :], scores[:, h % 2, qt, :], ACT.Exp,
                                                    bias=soft[:, h % 2, 0, qt:qt + 1],
                                                    accum_out=soft[:, h % 2, 1, qt:qt + 1])
                        if qt == 0:
                            link(last)
                    last.then_inc(exp_done.sem, 1)

                head_exp(0)
                head_exp(1)
                for h in range(NH):
                    gate(2 * h)
                    act.wait_ge(pT_done.sem, pT_done.at(l, h + 1))
                    nc.scalar.activation(probs_T[:, h % 2, :, :], bank[6][:, :].rearrange(
                        "p (k q) -> p k q", k=TT), ACT.Copy).then_inc(pT_ready.sem, 1)
                    gate(2 * h + 1)
                    if h + 2 < NH:
                        head_exp(h + 2)
                for tt in range(TT):
                    act.wait_ge(zt_done.sem, zt_done.at(l, tt + 1))
                    nc.scalar.activation(z_tok[:, tt, :], bank[4 + tt][:, :], ACT.Copy).then_inc(zt_ready.sem, 1)
                for n in range(T_UP, T_OUT):
                    tile_wait(n)
                for m in range(8):
                    if m < 7:
                        tile_wait(T_OUT + m)
                    if m % 2:
                        act.wait_ge(out_used.sem, out_used.at(l, m + 1))
                        square(2, m // 2)
                tile_wait(T_OUT + 7)
                act.dma_start(subk[:, :, :], subkeys[bass.ds(l, 1)].rearrange("a p m n -> (a p) m n")
                              ).then_inc(subk_in.sem, 16)
                norm_root(2)
                norm_high(2)
                with act.Fori(0, (T_U - T_WQ) // RING) as w:
                    for s in range(RING):
                        high_parts(l, w, T_WQ + s + AHEAD)
                        nc.scalar.activation(q2T[:, bass.ds(w * RING + s, 1), :].rearrange("p a t -> p (a t)"),
                                             bank[s % 4][:, 0:S], ACT.Copy).then_inc(tile_copied.sem, 1)
                for n in range(8):
                    tt, g = n // 4, n % 4
                    act.wait_ge(score_done.sem, score_done.at(l, n + 1))
                    nc.scalar.activation(s_all[:, tt, g * 512:(g + 1) * 512], bank[4 + g][:, :], ACT.Copy
                                         ).then_inc(score_copied.sem, 1)

                def gelus(first, count):
                    with act.Fori(0, count // RING) as i:
                        for s in range(RING):
                            high_parts(l, i, T_U + first + s + AHEAD)
                            nc.scalar.activation(experts[:, bass.ds(i * RING + (first + s), 1), :].rearrange(
                                "p a t -> p (a t)"), bank[s % 2][:, 0:S], ACT.Gelu_apprx_tanh
                                ).then_inc(gelu_done.sem, 1)

                load_table(ACT.Gelu_apprx_tanh)
                gelus(0, 48)
                act.wait_ge(best_ready.sem, best_ready.at(l, 1))
                nc.scalar.activation(expd[:, :, :], expd[:, :, :], ACT.Exp).then_inc(expd_ready.sem, 1)
                load_table(ACT.Gelu_apprx_tanh)
                gelus(48, 16)
                act.wait_ge(route_done.sem, route_done.at(l, 1))
                gelus(64, 60)

                def expert_high(i, n):
                    nc.scalar.activation(e_hi[:, n % AHEAD, :], experts[:, bass.ds(i * RING + n, 1), :].rearrange(
                        "p a t -> p (a t)"), ACT.Copy).then_inc(e_hi_ready.sem, 1)

                for n in range(NK - RING, NK):
                    if n == NK - 1:
                        act.wait_ge(g_used.sem, g_used.at(l, HALF))
                        expert_high(0, 0)
                    high_parts(l, 0, T_U + n + AHEAD)
                    nc.scalar.activation(experts[:, n, :], bank[n % 2][:, 0:S], ACT.Gelu_apprx_tanh
                                         ).then_inc(gelu_done.sem, 1)
                expert_high(0, 1)

                def v_parts(i, n):
                    act.wait_ge(tile_done.sem, tile_done.at(l, i * RING + (T_VT + n + 1)))
                    expert_high(i, n + AHEAD)
                    high_parts(l, i, T_VT + n + AHEAD)

                with act.Fori(0, HALF // RING - 1) as i:
                    for s in range(RING):
                        v_parts(i, s)
                for n in range(HALF - RING, HALF):
                    if n == HALF - AHEAD:
                        high_parts(l, 0, T_VT + n + AHEAD)
                        act.wait_ge(g_used.sem, g_used.at(l, 2 * HALF))
                        expert_high(0, n + AHEAD)
                    else:
                        v_parts(0, n)
                with act.Fori(0, HALF // RING - 1) as i:
                    for s in range(RING):
                        v_parts(i, HALF + s)
                for n in range(NK - RING, NK - AHEAD):
                    v_parts(0, n)

        @block.vector
        def _(dve):
            count = [0]
            V = nc.vector
            V.memset(zeros[:, :], 0.0)
            V.memset(eps_col[:, :], EPS)
            for b in range(KT // 2):
                dve.wait_ge(x_loaded[b], 16)
                V.drain().then_inc(trunk_in.sem, 1)
            dve.wait_ge(consts_in, 32)
            V.tensor_copy(iota_k[:, :], iota[:, 0:TOPK])
            V.tensor_copy(iota_t[:, :, :], iota[:, :].unsqueeze(2).to_broadcast([P, NK, TOK]))
            V.drain().then_inc(layer_chain, 1)

            with dve.Fori(0, DEPTH) as l:
                dve.drain()
                dve.sem_clear(dve_chain)

                def link(ins):
                    count[0] += 1
                    ins.then_inc(dve_chain, 1)
                    dve.wait_ge(dve_chain, count[0])

                def refine(tmp, src, n):
                    y0, t, y = tmp[0:n, 1, :], tmp[0:n, 0, :], tmp[0:n, 2, :]
                    link(V.reciprocal(y0, tmp[0:n, 0, :]))
                    link(V.scalar_tensor_tensor(t, y0, -0.5, y0, ALU.mult, ALU.mult))
                    link(V.scalar_tensor_tensor(t, src, EPS, t, ALU.add, ALU.mult))
                    return V.scalar_tensor_tensor(y, t, 1.5, y0, ALU.add, ALU.mult)

                def norm(n, gain):
                    dve.wait_ge(root_ready.sem, root_ready.at(l, n))
                    link(refine(norm_tmp, bank[3][:, 0:S], P))
                    first = (n - 1) * (KT // 2)
                    for b in range(KT // 2 + 1):
                        if b < KT // 2:
                            for k in (2 * b, 2 * b + 1):
                                ins = V.scalar_tensor_tensor(hT[:, k, :], xT[:, k, :], col[:, gain + k:gain + k + 1],
                                                             norm_tmp[:, 2, :], ALU.mult, ALU.mult)
                            ins.then_inc(h_made.sem, 1)
                        if b:
                            dve.wait_ge(h_hi_ready.sem, h_hi_ready.at(l, first + b))
                            two = slice(2 * b - 2, 2 * b)
                            V.tensor_tensor(act_lo[:, two, :], hT[:, two, :], act_hi[:, two, :].bitcast(F32),
                                            ALU.subtract).then_inc(h_ready.sem, 1)

                def two_parts(src, k, n):
                    link(V.tensor_copy(act_hi[:, k:k + n, :], src))
                    return V.tensor_tensor(act_lo[:, k:k + n, :], src, act_hi[:, k:k + n, :].bitcast(F32),
                                           ALU.subtract)

                def sine_argument(n, b):
                    f = slice(0, FFN)
                    dve.wait_ge(ffn_done.sem, ffn_done.at(l, n))
                    link(V.tensor_scalar(arg[f, :], bank[5][f, 0:S], ffn_col[f, b:b + 1], ffn_col[f, 1:2],
                                         ALU.add, ALU.mult))
                    link(V.tensor_scalar(turns[f, :], arg[f, :], 1.0 / (2.0 * math.pi), MAGIC, ALU.mult, ALU.add))
                    link(V.tensor_scalar(turns[f, :], turns[f, :], MAGIC, None, ALU.subtract))
                    link(V.scalar_tensor_tensor(arg[f, :], turns[f, :], -TWO_PI_HI, arg[f, :], ALU.mult, ALU.add))
                    link(V.scalar_tensor_tensor(arg[f, :], turns[f, :], -TWO_PI_LO, arg[f, :], ALU.mult, ALU.add))
                    V.tensor_scalar(arg[f, :], arg[f, :], PI_BELOW, -PI_BELOW, ALU.min, ALU.max
                                    ).then_inc(arg_ready.sem, 1)

                V.tensor_copy(col[:, :], all_cols[:, bass.ds(l, 1), :].rearrange("p a n -> p (a n)"))
                V.tensor_scalar(half_gate_b[:, :], all_cols[:, bass.ds(l, 1), C_GB:C_GB + 16].rearrange(
                    "p a n -> p (a n)"), 0.5, None, ALU.mult)
                V.memset(u_pad[:, :, 0:1], 0.0)
                V.memset(u_pad[:, :, S + 1:S + 2], 0.0).then_inc(setup_done.sem, 1)
                norm(1, C_G1)
                dve.wait_ge(net_in.sem, net_in.at(l, net_in.per_layer))
                f = slice(0, FFN)
                V.tensor_tensor(w3_sd[f, 0, :], w3[f, 0, :], w3[f, 1, :], ALU.add)
                V.tensor_tensor(w3_sd[f, 1, :], w3[f, 0, :], w3[f, 1, :], ALU.subtract
                                ).then_inc(w3_ready.sem, 1)
                def normalise_qk(n):
                    dve.wait_ge(spread_done.sem, spread_done.at(l, n + 1))
                    gain = C_QG if n < 2 else C_KG
                    V.scalar_tensor_tensor(qk_n[:, 2 * n:2 * n + 2, :].rearrange("p a t -> p (a t)"),
                                           qk_raw[:, 2 * n:2 * n + 2, :].rearrange("p a t -> p (a t)"),
                                           col[:, gain:gain + 1], bank[4 + n % 2][:, :], ALU.mult, ALU.mult
                                           ).then_inc(qk_ready.sem, 1)

                sine_argument(1, 0)
                dve.wait_ge(qk_root.sem, qk_root.at(l, 1))
                refine(qk_tmp, bank[4][0:2 * NH, 0:S], 2 * NH).then_inc(qk_scale_ready.sem, 1)
                dve.wait_ge(sin_done.sem, sin_done.at(l, 1))
                sine_argument(2, 2)
                for n in range(4):
                    normalise_qk(n)
                for n in range(4):
                    sd, tt = n // TT, n % TT
                    dve.wait_ge(taps_done.sem, taps_done.at(l, n + 1))
                    ins = V.tensor_tensor(filters[:, sd, tt, :], bank[4 + n][:, :], decay[:, tt, :], ALU.mult)
                    if n == 0:
                        link(ins)
                        ins = V.tensor_tensor(filters[0:1, 0, 0, :], filters[0:1, 0, 0, :],
                                              skip[0:1, :], ALU.add)
                    ins.then_inc(filters_ready.sem, 1)
                dve.wait_ge(tables_in.sem, tables_in.at(l, tables_in.per_layer))
                for h in range(NH):
                    ins = V.tensor_tensor(bias[:, h, :, :], bias[:, h, :, :],
                                          mask.unsqueeze(1).to_broadcast([P, TT, S]), ALU.add)
                link(ins)

                def conv(n):
                    dve.wait_ge(tile_copied.sem, tile_copied.at(l, 8 + n + 1))
                    w = C_CW + 3 * n
                    link(V.tensor_scalar(u[:, n, :], u_pad[:, n, 1:S + 1], col[:, w + 1:w + 2],
                                         col[:, C_CB + n:C_CB + n + 1], ALU.mult, ALU.add))
                    link(V.scalar_tensor_tensor(u[:, n, :], u_pad[:, n, 0:S], col[:, w:w + 1], u[:, n, :],
                                                ALU.mult, ALU.add))
                    link(V.scalar_tensor_tensor(u[:, n, :], u_pad[:, n, 2:S + 2], col[:, w + 2:w + 3], u[:, n, :],
                                                ALU.mult, ALU.add))

                def head_scores(h):
                    dve.wait_ge(scores_done.sem, scores_done.at(l, h + 1))
                    link(V.scalar_tensor_tensor(scores[:, h % 2, :, :].rearrange("p a t -> p (a t)"),
                                                bank[4 + h % 2][:, :], HD ** -0.5,
                                                bias[:, h, :, :].rearrange("p a t -> p (a t)"),
                                                ALU.mult, ALU.add))
                    V.tensor_reduce(soft[:, h % 2, 0, :], scores[:, h % 2, :, :], AX, ALU.max, negate=True
                                    ).then_inc(scores_ready.sem, 1)

                head_scores(0)
                head_scores(1)
                tiles = [4, 8, 5, 9, 6, 10, 7, 11, 0, 1, 2, 3]
                for h in range(NH):
                    dve.wait_ge(exp_done.sem, exp_done.at(l, h + 1))
                    link(V.reciprocal(soft[:, h % 2, 2, :], soft[:, h % 2, 1, :]))
                    for qt in range(TT):
                        ins = V.tensor_scalar(probs[:, h % 2, qt, :], probs[:, h % 2, qt, :],
                                              soft[:, h % 2, 2, qt:qt + 1], None, ALU.mult)
                        if qt == 0:
                            link(ins)
                    ins.then_inc(probs_ready.sem, 1)
                    for _ in range(2 - h % 2):
                        conv(tiles.pop(0))
                    if h == 4:
                        V.tensor_tensor(zT[:, :, :], u[:, 4:8, :], u[:, 8:12, :], ALU.mult
                                        ).then_inc(z_ready.sem, 1)
                    if h + 2 < NH:
                        head_scores(h + 2)
                    if h == NH - 1:
                        dve.wait_ge(tile_done.sem, tile_done.at(l, T_UP))
                        dve.wait_ge(attn_ready.sem, attn_ready.at(l, h // 2))
                        two_parts(attn_T[:, 0:3, :], 0, 3).then_inc(attn_split.sem, 1)
                    if h % 2:
                        dve.wait_ge(pv_done.sem, pv_done.at(l, h + 1))
                        V.tensor_copy(attn_T[:, h // 2, :], bank[7][:, 0:S]).then_inc(attn_ready.sem, 1)
                dve.wait_ge(attn_ready.sem, attn_ready.at(l, NH // 2))
                two_parts(attn_T[:, 3:4, :], 3, 1).then_inc(attn_split.sem, 1)

                def times_spectrum(f):
                    re, im = (bank[6], bank[7]) if f == 0 else (bank[4], bank[5])
                    dve.wait_ge(zf_done.sem, zf_done.at(l, f + 1))
                    if f:
                        dve.wait_ge(y_ready.sem, y_ready.at(l, f))
                    V.tensor_tensor(prod[:, 0, :], re[:, :], spectrum[:, 0, f, :], ALU.mult)
                    link(V.tensor_tensor(prod[:, 1, :], im[:, :], spectrum[:, 1, f, :], ALU.mult))
                    link(V.tensor_tensor(spec_y[:, 0, f, :], prod[:, 0, :], prod[:, 1, :], ALU.subtract))
                    V.tensor_tensor(prod[:, 0, :], re[:, :], spectrum[:, 1, f, :], ALU.mult)
                    link(V.tensor_tensor(prod[:, 1, :], im[:, :], spectrum[:, 0, f, :], ALU.mult))
                    V.tensor_tensor(spec_y[:, 1, f, :], prod[:, 0, :], prod[:, 1, :], ALU.add
                                    ).then_inc(y_ready.sem, 1)

                def gated_attention(m):
                    dve.wait_ge(tile_done.sem, tile_done.at(l, T_UP + m // 2 + 1))
                    V.scalar_tensor_tensor(merged[:, m, :], gates[:, m, :], 1.0, bank[m % 4][:, 0:S],
                                           ALU.add, ALU.mult).then_inc(up_used.sem, 1)

                def gated_hyena(m):
                    dve.wait_ge(tile_done.sem, tile_done.at(l, T_UP + 4 + m // 2 + 1))
                    link(V.scalar_tensor_tensor(prod[:, m % 2, 0:S], gates[:, 8 + m, :], 1.0, bank[m % 4][:, 0:S],
                                                ALU.add, ALU.mult))
                    V.tensor_tensor(merged[:, m, :], merged[:, m, :], prod[:, m % 2, 0:S], ALU.add
                                    ).then_inc(up_used.sem, 1)

                def merged_parts(k):
                    dve.wait_ge(up_used.sem, up_used.at(l, 8 + k + 2))
                    two_parts(merged[:, k:k + 2, :], k, 2).then_inc(merged_split.sem, 1)

                times_spectrum(0)
                gated_attention(0)
                gated_attention(1)
                times_spectrum(1)
                for m in range(2, 6):
                    gated_attention(m)
                for ct in range(4):
                    dve.wait_ge(conv_done.sem, conv_done.at(l, 2 * (ct // 2) + 2))
                    link(V.tensor_tensor(hyena_T[:, ct, :], bank[6 + ct // 2][:, (ct % 2) * S:(ct % 2 + 1) * S],
                                         u[:, ct, :], ALU.mult))
                    two_parts(hyena_T[:, ct:ct + 1, :], 4 + ct, 1).then_inc(hyena_ready.sem, 1)
                gated_attention(6)
                gated_attention(7)
                for m in range(4):
                    gated_hyena(m)
                    if m % 2:
                        merged_parts(m - 1)
                gated_hyena(4)
                gated_hyena(5)
                dve.wait_ge(tile_done.sem, tile_done.at(l, T_OUT))
                merged_parts(4)
                gated_hyena(6)
                gated_hyena(7)
                merged_parts(6)
                for m in range(8):
                    dve.wait_ge(tile_done.sem, tile_done.at(l, T_OUT + m + 1))
                    V.scalar_tensor_tensor(xT[:, m, :], bank[4 + m % 4][:, 0:S], 0.5, xT[:, m, :],
                                           ALU.mult, ALU.add).then_inc(out_used.sem, 1)
                norm(2, C_G2)

                taken = [0]
                with dve.Fori(0, TT) as tt:
                    dve.drain()
                    dve.sem_clear(route_chain)

                    def step(ins):
                        taken[0] += 1
                        ins.then_inc(route_chain, 1)
                        dve.wait_ge(route_chain, taken[0])

                    dve.wait_ge(score_copied.sem, tt * 4 + score_copied.at(l, 4))
                    step(V.tensor_copy(s_cur[:, :, :].rearrange("p a b -> p (a b)"),
                                       s_all[:, bass.ds(tt, 1), :].rearrange("p a b -> p (a b)")))
                    for m in range(2 * PH):
                        step(V.max(top_s[:, m, 0:8], s_cur[:, m, :]))
                        V.max_index(top_i[:, m, 0:8], top_s[:, m, 0:8], s_cur[:, m, :])
                        step(V.match_replace(s_rest[:, m, :], top_s[:, m, 0:8], s_cur[:, m, :], LOWEST))
                        step(V.max(top_s[:, m, 8:16], s_rest[:, m, :]))
                        V.max_index(top_i[:, m, 8:16], top_s[:, m, 8:16], s_rest[:, m, :])
                    sides = top_s[:, :, :].rearrange("p (h s) k -> p h s k", s=2)
                    wide = [P, PH, TOPK, TOPK]
                    step(V.tensor_tensor(cand[:, :, :, :], sides[:, :, 0, :].unsqueeze(3).to_broadcast(wide),
                                         sides[:, :, 1, :].unsqueeze(2).to_broadcast(wide), ALU.add))
                    for h in range(PH):
                        c = cand[:, h, :, :].rearrange("p a b -> p (a b)")
                        b0, b1 = best_s[:, h * TOPK:h * TOPK + 8], best_s[:, h * TOPK + 8:h * TOPK + 16]
                        step(V.max(b0, c))
                        V.max_index(best_i[:, h, 0:8], b0, c)
                        step(V.match_replace(cand_rest[:, h, :], b0, c, LOWEST))
                        step(V.max(b1, cand_rest[:, h, :]))
                        step(V.max_index(best_i[:, h, 8:16], b1, cand_rest[:, h, :]))
                    flat_i = best_i[:, :, :].rearrange("p h k -> p (h k)")
                    V.tensor_scalar(rank[:, 0, :], flat_i, 4, None, ALU.logical_shift_right)
                    step(V.tensor_scalar(rank[:, 1, :], flat_i, TOPK - 1, None, ALU.bitwise_and))
                    V.tensor_copy(rank_f[:, :, :], rank[:, :, :])
                    V.tensor_copy(best_all[:, bass.ds(tt, 1), :].rearrange("p a k -> p (a k)"), best_s[:, :])
                    step(V.tensor_copy(top_if[:, :, :, :].rearrange("p h s k -> p (h s) k"), top_i[:, :, :]))
                    for side in range(2):
                        shape3 = [P, PH * TOPK, TOPK]
                        step(V.tensor_tensor(pick[:, :, :], rank_f[:, side, :].unsqueeze(2).to_broadcast(shape3),
                                             iota_k[:, :].unsqueeze(1).to_broadcast(shape3), ALU.is_equal))
                        pick4 = pick[:, :, :].rearrange("p (h k) a -> p h k a", h=PH)
                        step(V.tensor_tensor(pick4, pick4,
                                             top_if[:, :, side, :].unsqueeze(2).to_broadcast(wide), ALU.mult))
                        step(V.tensor_reduce(slots[:, bass.ds(tt, 1), side, :].rearrange("p a k -> p (a k)"),
                                             pick[:, :, :], AX, ALU.add))
                best_v = best_all[:, :, :].rearrange("p t (h k) -> p (t h) k", k=TOPK)
                expd_v = expd[:, :, :].rearrange("p t (h k) -> p (t h) k", k=TOPK)
                shape = [P, TT * PH, TOPK]
                V.tensor_tensor(expd_v, best_v, best_v[:, :, 0:1].to_broadcast(shape), ALU.subtract
                                ).then_inc(best_ready.sem, 1)
                dve.wait_ge(expd_ready.sem, expd_ready.at(l, 1))
                den = top_if[:, :, :, :].rearrange("p a b c -> p (a b c)")
                link(V.tensor_reduce(den[:, 0:16], expd_v, AX, ALU.add))
                link(V.reciprocal(den[:, 16:32], den[:, 0:16]))
                for tt in range(TT):
                    ins = V.tensor_tensor(slots[:, tt, 2, :].rearrange("p (h k) -> p h k", k=TOPK),
                                          expd[:, tt, :].rearrange("p (h k) -> p h k", k=TOPK),
                                          den[:, 16 + 8 * tt:24 + 8 * tt].unsqueeze(2).to_broadcast([P, PH, TOPK]),
                                          ALU.mult)
                ins.then_inc(slots_ready.sem, 1)
                for tt in range(TT):
                    dve.wait_ge(slotT_done.sem, slotT_done.at(l, tt + 1))
                    cols_ = slice(tt * P, (tt + 1) * P)
                    src = bank[2 + tt][:, 0:3 * P].rearrange("p (c t) -> p c t", c=3)
                    link(V.tensor_copy(slotT[:, 0:3, cols_], src))
                    link(V.tensor_tensor(w_rest[:, :], src[:, 2, :], slotT[:, 2, cols_], ALU.subtract))
                    link(V.tensor_copy(slotT[:, 3, cols_], w_rest[:, :]))
                    link(V.tensor_tensor(w_rest[:, :], w_rest[:, :], slotT[:, 3, cols_], ALU.subtract))
                    ins = V.tensor_copy(slotT[:, 4, cols_], w_rest[:, :])
                    if tt == 0:
                        link(ins)
                ins.then_inc(route_done.sem, 1)

                def one_hots(half, i, n):
                    tokens = bass.ds(i * (RING * TOK) + n * TOK, TOK)

                    def over_keys(c, n_keys):
                        return slotT[:, c, tokens].unsqueeze(1).to_broadcast([P, n_keys, TOK])

                    V.tensor_tensor(onehot_j[:, n % 2, :, :], iota_t[:, half * HALF:(half + 1) * HALF, :],
                                    over_keys(1, HALF), ALU.is_equal).then_inc(onehot_chain, 1)
                    V.tensor_tensor(onehot_i[:, n % 2, :, :], iota_t[:, :, :], over_keys(0, NK), ALU.is_equal)
                    built[0] += 1
                    dve.wait_ge(onehot_chain, built[0])
                    V.tensor_tensor(weighted_j[:, n % 2, :, :, :],
                                    onehot_j[:, n % 2, :, :].unsqueeze(1).to_broadcast([P, 3, HALF, TOK]),
                                    slotT[:, 2:5, tokens].unsqueeze(2).to_broadcast([P, 3, HALF, TOK]),
                                    ALU.mult).then_inc(onehot_ready.sem, 1)

                def weight_experts(half, i, n):
                    if n % RING == 0:
                        dve.wait_ge(gelu_done.sem, gelu_done.at(l, (half + 1) * HALF))
                    dve.wait_ge(g_done.sem, g_done.at(l, i * RING + (half * HALF + n + 1)))
                    tokens = bass.ds(i * (RING * TOK) + n * TOK, TOK)
                    w = experts[:, half * HALF:(half + 1) * HALF, tokens]
                    V.tensor_tensor(w, w, bank[2 + n % 2][:, 0:TOK * HALF].rearrange("p (t j) -> p j t", t=TOK),
                                    ALU.mult).then_inc(g_used.sem, 1)

                def pair(half, i, n):
                    for m in (n, n + 1):
                        weight_experts(half, i, m)
                    for m in (n + 2, n + 3):
                        if m < HALF:
                            one_hots(half, i, m)
                        elif half == 0:
                            one_hots(1, 0, m - HALF)
                    if half == 0 and n == 0:
                        dve.wait_ge(lo_ready[0].sem, lo_ready[0].at(l, POOL_TILES))
                    for m in (n, n + 1):
                        low_parts(V, l, i, POOL_TILES + half * HALF + m, [0])

                built = [0]
                dve.drain()
                dve.sem_clear(onehot_chain)
                one_hots(0, 0, 0)
                one_hots(0, 0, 1)
                for half in range(2):
                    with dve.Fori(0, HALF // RING - 1) as i:
                        dve.drain()
                        dve.sem_clear(onehot_chain)
                        built = [0]
                        for s in range(0, RING, 2):
                            pair(half, i, s)
                    dve.drain()
                    dve.sem_clear(onehot_chain)
                    built = [0]
                    for n in range(HALF - RING, HALF, 2):
                        pair(half, 0, n)
                with dve.Fori(0, HALF // RING - 1) as i:
                    for s in range(RING):
                        low_parts(V, l, i, T_VT + HALF + s + AHEAD, [0])
                for n in range(TILES - RING + AHEAD, TILES):
                    low_parts(V, l, 0, n, [0])
                V.drain().then_inc(layer_chain, 1)
                dve.wait_ge(tile_done.sem, tile_done.at(l, TILES))
                for b in range(4):
                    V.tensor_tensor(xT[:, 2 * b:2 * b + 2, :].rearrange("p a t -> p (a t)"), bank[4 + b][:, :],
                                          xT[:, 2 * b:2 * b + 2, :].rearrange("p a t -> p (a t)"), ALU.add
                                    ).then_inc(trunk_in.sem, 1)

        @block.tensor
        def _(pe):
            T = nc.tensor

            with pe.Fori(0, DEPTH) as l:
                def parts_ready(i, tile, half):
                    pe.wait_ge(lo_ready[half].sem, lo_ready[half].at(l, i * RING + (tile + 1)))

                def weights(part_, tile, k):
                    return part_[:, 2 * (tile % AHEAD) + k // 4, (k % 4) * P:(k % 4 + 1) * P]

                def product(out_, tile, j, k, start, stop):
                    T.matmul(out_, weights(w_hi, tile, j), act_hi[:, k, :], start=start, stop=False,
                             skip_group_check=True)
                    T.matmul(out_, weights(w_hi, tile, j), act_lo[:, k, :], start=False, stop=False,
                             skip_group_check=True)
                    return T.matmul(out_, weights(w_lo, tile, j), act_hi[:, k, :], start=False, stop=stop,
                                    skip_group_check=True)

                def contract(out_, i, tile, wait=None):
                    for k in range(KT):
                        if k % 4 == 0:
                            parts_ready(i, tile, k // 4)
                        if wait is not None:
                            wait(k)
                        ins = product(out_, tile, k, k, k == 0, k == KT - 1)
                    return ins

                def trunk_part(n):
                    def wait(k):
                        if k % 2 == 0:
                            pe.wait_ge(h_ready.sem, h_ready.at(l, (n - 1) * (KT // 2) + k // 2 + 1))
                    return wait

                def project(tile, m, wait=None):
                    if m >= 4:
                        pe.wait_ge(tile_copied.sem, tile_copied.at(l, m - 3))
                    contract(bank[m % 4][:, 0:S], 0, tile, wait=wait).then_inc(tile_done.sem, 1)

                def mean_square(n, b):
                    pe.wait_ge(sq_ready.sem, sq_ready.at(l, (n - 1) * (KT // 2) + b + 1))
                    for k in (2 * b, 2 * b + 1):
                        ins = T.matmul(bank[3][:, 0:S], mean_all, squares[:, k, :], start=(k == 0),
                                       stop=(k == KT - 1), skip_group_check=True)
                    if b == KT // 2 - 1:
                        ins.then_inc(ms_done.sem, 1)

                def spread_scale(n):
                    for m in (2 * n, 2 * n + 1):
                        ins = T.matmul(bank[4 + n % 2][:, (m % 2) * S:(m % 2 + 1) * S], spread[0:2 * NH, m, :],
                                       qk_tmp[0:2 * NH, 2, :], start=True, stop=True)
                    ins.then_inc(spread_done.sem, 1)

                pe.wait_ge(mats_loaded, 16)
                for b in range(KT // 2):
                    mean_square(1, b)
                for m in range(8):
                    if m == 7:
                        pe.wait_ge(net_in.sem, net_in.at(l, net_in.per_layer))
                    project(T_QK + m, m, trunk_part(1) if m == 0 else None)
                T.matmul(bank[5][0:FFN, 0:S], w1[0:POS, :], pos[0:POS, :], start=True, stop=True
                         ).then_inc(ffn_done.sem, 1)
                for n in range(4):
                    if n == 1:
                        pe.wait_ge(tile_copied.sem, tile_copied.at(l, 8))
                        for m in range(8):
                            ins = T.matmul(bank[4][0:2 * NH, 0:S], by_head[:, m * 2 * NH:(m + 1) * 2 * NH],
                                           qk_sq[:, m, :], start=(m == 0), stop=(m == 7))
                        ins.then_inc(ss_done.sem, 1)
                    if n == 3:
                        pe.wait_ge(arg_ready.sem, arg_ready.at(l, 1))
                        pe.wait_ge(sin_done.sem, sin_done.at(l, 1))
                    for half in range(2):
                        parts_ready(0, T_V + n, half)
                        k, part_ = 2 * n + half, 2 * (n % AHEAD) + half
                        for tt in range(TT):
                            tokens = slice(tt * P, (tt + 1) * P)
                            T.matmul(bank[6 + tt][:, :], act_hi[:, k, tokens], w_hi[:, part_, :],
                                     start=(k == 0), stop=False)
                            T.matmul(bank[6 + tt][:, :], act_hi[:, k, tokens], w_lo[:, part_, :],
                                     start=False, stop=False)
                            ins = T.matmul(bank[6 + tt][:, :], act_lo[:, k, tokens], w_hi[:, part_, :],
                                           start=False, stop=(k == KT - 1))
                    ins.then_inc(tile_done.sem, 1)
                    if n == 3:
                        T.matmul(bank[5][0:FFN, 0:S], w2[0:FFN, :], h1[0:FFN, :], start=True, stop=True
                                 ).then_inc(ffn_done.sem, 1)
                project(T_HY, 8)
                pe.wait_ge(qk_scale_ready.sem, qk_scale_ready.at(l, 1))
                spread_scale(0)
                project(T_HY + 1, 9)
                pe.wait_ge(arg_ready.sem, arg_ready.at(l, 2))
                spread_scale(1)
                project(T_HY + 2, 10)
                for n in (2, 3):
                    pe.wait_ge(qk_ready.sem, qk_ready.at(l, n - 1))
                    spread_scale(n)
                project(T_HY + 3, 11)
                pe.wait_ge(sin_done.sem, sin_done.at(l, 2))
                pe.wait_ge(w3_ready.sem, w3_ready.at(l, 1))
                pe.wait_ge(qk_ready.sem, qk_ready.at(l, 4))
                pe.wait_ge(v_ready.sem, v_ready.at(l, 2))
                for n in range(4):
                    sd, tt = n // TT, n % TT
                    T.matmul(bank[4 + n][:, :], h2[0:FFN, tt * P:(tt + 1) * P], w3_sd[0:FFN, sd, :],
                             start=True, stop=True).then_inc(taps_done.sem, 1)
                for n in range(4, 7):
                    project(T_HY + n, 8 + n)
                pe.wait_ge(filters_ready.sem, filters_ready.at(l, 4))
                pe.wait_ge(tables_in.sem, tables_in.at(l, tables_in.per_layer))
                for n in range(4):
                    ri, f = n // TT, n % TT
                    for k in range(TT):
                        ins = T.matmul(bank[4 + n][:, :], dft[:, ri, k, f * P:(f + 1) * P], filters[:, ri, k, :],
                                       start=(k == 0), stop=(k == TT - 1))
                    ins.then_inc(spec_done.sem, 1)

                def head_scores(h):
                    r0, m = (h % 2) * HD, h // 2
                    if h >= 2:
                        pe.wait_ge(scores_ready.sem, scores_ready.at(l, h - 1))
                    for qt in range(TT):
                        ins = T.matmul(bank[4 + h % 2][:, qt * S:(qt + 1) * S],
                                       qk_n[r0:r0 + HD, m, qt * P:(qt + 1) * P], qk_n[r0:r0 + HD, 4 + m, :],
                                       start=True, stop=True)
                    ins.then_inc(scores_done.sem, 1)

                project(T_HY + 7, 15)
                project(T_HY + 8, 16)
                pe.wait_ge(spec_ready.sem, spec_ready.at(l, 4))
                head_scores(0)
                head_scores(1)
                project(T_HY + 9, 17)
                project(T_HY + 10, 18)
                project(T_HY + 11, 19)
                for h in range(NH):
                    project(T_GATE + 2 * h, 20 + 2 * h)
                    pe.wait_ge(probs_ready.sem, probs_ready.at(l, h + 1))
                    if h:
                        pe.wait_ge(pT_ready.sem, pT_ready.at(l, h))
                    for qt in range(TT):
                        for kt in range(TT):
                            ins = T.transpose(bank[6][:, kt * S + qt * P:kt * S + (qt + 1) * P],
                                              probs[:, h % 2, qt, kt * P:(kt + 1) * P], identity)
                    ins.then_inc(pT_done.sem, 1)
                    project(T_GATE + 2 * h + 1, 20 + 2 * h + 1)
                    pe.wait_ge(pT_ready.sem, pT_ready.at(l, h + 1))
                    if h >= 2 and h % 2 == 0:
                        pe.wait_ge(attn_ready.sem, attn_ready.at(l, h // 2))
                    r0 = (h % 2) * HD
                    for kt in range(TT):
                        ins = T.matmul(bank[7][r0:r0 + HD, 0:S], v_tok[:, kt, h * HD:(h + 1) * HD],
                                       probs_T[:, h % 2, kt, :], start=(kt == 0), stop=(kt == TT - 1))
                    ins.then_inc(pv_done.sem, 1)
                    if h + 2 < NH:
                        head_scores(h + 2)
                pe.wait_ge(z_ready.sem, z_ready.at(l, 1))
                for tt in range(TT):
                    for ct in range(4):
                        ins = T.transpose(bank[4 + tt][:, ct * P:(ct + 1) * P], zT[:, ct, tt * P:(tt + 1) * P],
                                          identity)
                    ins.then_inc(zt_done.sem, 1)

                def up(n, wait=None):
                    for j in (0, 1):
                        m = 2 * n + j
                        if m < 4:
                            pe.wait_ge(tile_copied.sem, tile_copied.at(l, 36))
                        else:
                            pe.wait_ge(up_used.sem, up_used.at(l, m - 3))
                        parts_ready(0, T_UP + n, j)
                        for k in range(4):
                            if wait is not None:
                                wait(k)
                            first = 4 * (n // 4)
                            ins = product(bank[m % 4][:, 0:S], T_UP + n, 4 * j + k, first + k, k == 0, k == 3)
                    ins.then_inc(tile_done.sem, 1)

                up(0, lambda k: pe.wait_ge(attn_split.sem, attn_split.at(l, 1 + k // 3)))
                pe.wait_ge(zt_ready.sem, zt_ready.at(l, TT))
                for f in range(TT):
                    for ri in range(2):
                        b = (bank[6], bank[7])[ri] if f == 0 else (bank[4], bank[5])[ri]
                        for k in range(TT):
                            ins = T.matmul(b[:, :], dft[:, ri, k, f * P:(f + 1) * P], z_tok[:, k, :],
                                           start=(k == 0), stop=(k == TT - 1))
                    ins.then_inc(zf_done.sem, 1)
                up(1)
                up(2)
                pe.wait_ge(y_ready.sem, y_ready.at(l, TT))
                for ct in range(4):
                    for ri in range(2):
                        for f in range(TT):
                            ins = T.matmul(bank[6 + ct // 2][:, (ct % 2) * S:(ct % 2 + 1) * S],
                                           spec_y[:, ri, f, ct * P:(ct + 1) * P], dft[:, 2 + ri, f, :],
                                           start=(ri == 0 and f == 0), stop=(ri == 1 and f == TT - 1))
                    ins.then_inc(conv_done.sem, 1)
                up(3)
                up(4, lambda k: pe.wait_ge(hyena_ready.sem, hyena_ready.at(l, k + 1)))
                for n in range(5, 8):
                    up(n)

                for k0 in (0, 4):
                    for m in range(2):
                        parts_ready(0, T_OUT + m, k0 // 4)
                        for k in range(k0, k0 + 4):
                            if m == 0 and k % 2 == 0:
                                pe.wait_ge(merged_split.sem, merged_split.at(l, k // 2 + 1))
                            ins = product(bank[4 + m][:, 0:S], T_OUT + m, k, k, k == 0, k == 7)
                        if k0:
                            ins.then_inc(tile_done.sem, 1)
                for m in range(2, 8):
                    if m >= 4:
                        pe.wait_ge(out_used.sem, out_used.at(l, m - 3))
                    contract(bank[4 + m % 4][:, 0:S], 0, T_OUT + m).then_inc(tile_done.sem, 1)
                    if m in (3, 5):
                        mean_square(2, m // 2 - 1)
                mean_square(2, 2)
                mean_square(2, 3)
                for s in range(RING):
                    contract(bank[s % 4][:, 0:S], 0, T_WQ + s, wait=trunk_part(2) if s == 0 else None
                             ).then_inc(tile_done.sem, 1)
                with pe.Fori(1, (T_U - T_WQ) // RING) as w:
                    for s in range(RING):
                        pe.wait_ge(tile_copied.sem, tile_copied.at(l, w * RING + (36 + s - 3)))
                        contract(bank[s % 4][:, 0:S], w, T_WQ + s).then_inc(tile_done.sem, 1)
                pe.wait_ge(subk_in.sem, subk_in.at(l, 16))
                for n in range(8):
                    tt, g = n // 4, n % 4
                    if n < 4:
                        pe.wait_ge(tile_copied.sem, tile_copied.at(l, 36 + 4 * (g + 1)))
                    else:
                        pe.wait_ge(score_copied.sem, score_copied.at(l, n - 3))
                    for c in range(4):
                        m = 4 * g + c
                        ins = T.matmul(bank[4 + g][:, c * P:(c + 1) * P], q2T[:, m, tt * P:(tt + 1) * P],
                                       subk[:, m, :], start=True, stop=True)
                    ins.then_inc(score_done.sem, 1)

                def u_tile(i, s, first):
                    if first + s >= 2:
                        pe.wait_ge(gelu_done.sem, gelu_done.at(l, i * RING + (first + s - 1)))
                    contract(bank[s % 2][:, 0:S], i, T_U + first + s).then_inc(tile_done.sem, 1)

                def routing_weights(i, s, half):
                    pe.wait_ge(onehot_ready.sem, onehot_ready.at(l, i * RING + (half * HALF + s + 1)))
                    for t in range(TOK):
                        for c in range(3):
                            ins = T.matmul(bank[2 + s % 2][:, t * HALF:(t + 1) * HALF], onehot_i[:, s % 2, :, t],
                                           weighted_j[:, s % 2, c, :, t], start=(c == 0), stop=(c == 2))
                    ins.then_inc(g_done.sem, 1)

                def v_tile(i, s, first, last=False):
                    pe.wait_ge(e_lo_ready.sem, e_lo_ready.at(l, i * RING + (first + s + 1)))
                    tile = T_VT + first + s
                    for ct in range(KT):
                        if ct % 4 == 0:
                            parts_ready(i, tile, ct // 4)
                        for w_, e_ in ((w_hi, e_hi), (w_hi, e_lo), (w_lo, e_hi)):
                            ins = T.matmul(bank[4 + ct // 2][:, (ct % 2) * S:(ct % 2 + 1) * S], weights(w_, tile, ct),
                                           e_[:, s % AHEAD, :], start=False, stop=last and w_ is w_lo,
                                           skip_group_check=True)
                    ins.then_inc(tile_done.sem, 1)

                for s in range(RING):
                    u_tile(0, s, 0)
                with pe.Fori(0, ROUTED // RING - 1) as i:
                    for s in range(RING):
                        u_tile(i, s, RING)
                pe.wait_ge(slots_ready.sem, slots_ready.at(l, 1))
                for tt in range(TT):
                    for c in range(3):
                        ins = T.transpose(bank[2 + tt][:, c * P:(c + 1) * P], slots[:, tt, c, :], identity)
                    ins.then_inc(slotT_done.sem, 1)
                pe.wait_ge(score_copied.sem, score_copied.at(l, 8))
                for b in range(4):
                    T.matmul(bank[4 + b][:, :], zeros[:, 0:P], zeros[:, :], start=True, stop=False,
                             skip_group_check=True)
                with pe.Fori(0, (HALF - ROUTED) // RING) as i:
                    for s in range(RING):
                        u_tile(i, s, ROUTED)
                with pe.Fori(0, HALF // RING) as i:
                    for s in range(0, RING, 2):
                        for m in (s, s + 1):
                            routing_weights(i, m, 0)
                        for m in (s, s + 1):
                            u_tile(i, m, HALF)
                with pe.Fori(0, HALF // RING) as i:
                    for s in range(0, RING, 2):
                        for m in (s, s + 1):
                            routing_weights(i, m, 1)
                        for m in (s, s + 1):
                            v_tile(i, m, 0)
                with pe.Fori(0, HALF // RING - 1) as i:
                    for s in range(RING):
                        v_tile(i, s, HALF)
                for s in range(RING - 1):
                    v_tile(0, s, NK - RING)
                v_tile(0, RING - 1, NK - RING, last=True)


def constants():
    f32 = np.float32
    t = np.linspace(0.0, 1.0, S, dtype=f32)[:, None]
    w = (2.0 * math.pi * np.arange(S, dtype=f32)[:, None] / S).astype(f32)
    f = np.linspace(1e-4, BANDS - 1, BANDS, dtype=f32)[None, :]
    pos = np.concatenate([t, np.cos(f * w), -np.sin(f * w)], axis=-1).astype(f32)
    lo, hi = math.log(1e-2) / 1.5, math.log(1e-2) / 0.3
    deltas = np.linspace(lo, hi, HW, dtype=f32)
    decay = np.exp(-t * np.abs(deltas)[None, :]).astype(f32)
    theta = np.outer(np.arange(S), np.arange(S) + 0.5) * (2.0 * math.pi / (2 * S))
    ahead = np.stack([np.cos(theta), -np.sin(theta)])
    back = np.stack([np.cos(theta.T), -np.sin(theta.T)]) / S
    dft = np.concatenate([ahead, back]).astype(f32).reshape(4, TT, P, S).transpose(2, 0, 1, 3)
    c = np.arange(GRID_W)
    c0 = np.clip(c - KW // 2, 0, GRID_W - KW)
    inside = (c[None, :] >= c0[:, None]) & (c[None, :] < c0[:, None] + KW)
    mask = np.tile(np.where(inside, 0.0, -1e30).astype(f32), (2, ROWS))
    heads = np.zeros((P, KT, 2 * NH))
    for m in range(KT):
        for half in range(2):
            heads[half * HD:(half + 1) * HD, m, 2 * m + half] = 1.0
    mats = np.stack([np.eye(P), np.full((P, P), 1.0 / D), heads.reshape(P, P) / HD], axis=1).astype(f32)
    iota = np.tile(np.arange(P, dtype=f32), (P, 1))
    return {
        "pos_in": np.ascontiguousarray(pos.T), "dft_in": np.ascontiguousarray(dft),
        "decay_in": np.ascontiguousarray(decay.reshape(TT, P, HW).transpose(1, 0, 2)),
        "spread_in": np.ascontiguousarray(heads.transpose(2, 1, 0)).astype(f32), "mask_in": mask, "mats_in": mats, "iota_in": iota,
    }


def by_tiles(w):
    k, m = w.shape
    return w.reshape(k // P, P, m // P, P).transpose(2, 1, 0, 3).reshape(m // P, P, k)


def layer_stream(l, w_in, w_up_na, w_up_hy, w_out, peer_wq, peer_u, peer_v):
    na, hy = NH * HD, HW
    v = w_in[l][:, 2 * na:3 * na].reshape(4, 2, P, na).transpose(0, 2, 1, 3).reshape(4, P, D)
    up = [by_tiles(w[l]).reshape(4, 2, P, HW).transpose(0, 2, 1, 3).reshape(4, P, D) for w in (w_up_na, w_up_hy)]
    ut = peer_u[l].reshape(NK, NK, KT, P).transpose(1, 3, 2, 0).reshape(NK, P, D)
    vt = peer_v[l].reshape(NK, NK, D).transpose(1, 0, 2)
    return [by_tiles(w_in[l][:, 0:2 * na]), v, by_tiles(w_in[l][:, 3 * na:3 * na + 3 * hy]),
            by_tiles(w_in[l][:, 3 * na + 3 * hy:]), *up, by_tiles(w_out[l]), by_tiles(peer_wq[l]),
            ut, vt]


def kernel(**inputs):
    import concourse.bacc as bacc
    from concourse.bass_utils import run_bass_kernel_spmd

    a = {k: np.asarray(v) for k, v in inputs.items()}
    tiles = []
    for l in range(DEPTH):
        tiles += layer_stream(l, *(a[n] for n in ("w_in", "w_up_na", "w_up_hy", "w_out", "peer_wq",
                                                  "peer_u", "peer_v")))

    def column(v):
        return v.reshape(DEPTH, -1, P).transpose(0, 2, 1)

    gate_b = a["gate_b"].reshape(DEPTH, 2 * D)
    taps = a["hy_conv_w"].reshape(DEPTH, 3, 12, P).transpose(0, 3, 2, 1).reshape(DEPTH, P, 36)
    cols = np.concatenate([
        column(a["norm1_g"]), column(a["norm2_g"]), column(gate_b),
        np.tile(a["na_q_g"], (1, 2))[:, :, None], np.tile(a["na_k_g"], (1, 2))[:, :, None],
        taps, column(a["hy_conv_b"])], axis=2)
    c = np.arange(GRID_W)
    dc = np.clip(c[None, :] - c[:, None] + KW - 1, 0, 2 * KW - 2)
    dr = np.arange(KR_MAX - ROWS, KR_MAX + ROWS - 1)
    rpb = a["na_rpb"][:, :, dr][:, :, :, dc].transpose(0, 3, 1, 2, 4)
    arrays = {
        "x_in": a["x"][0].T.reshape(KT, P, S).transpose(1, 0, 2),
        "stream": np.concatenate(tiles, axis=0),
        "subkeys": a["peer_subkeys"].reshape(DEPTH, 2 * PH, NK, P).transpose(0, 3, 1, 2),
        "cols": cols.transpose(1, 0, 2),
        "ffn_cols": np.stack([a["hy_b1"], a["hy_freq"], a["hy_b2"]], axis=2),
        "w1_in": a["hy_w1"], "w2_in": a["hy_w2"], "w3_in": a["hy_w3"].reshape(DEPTH, FFN, 2, HW),
        "skip_in": a["hy_bias"], "rpb_in": rpb, **constants(),
    }
    arrays = {k: np.ascontiguousarray(v) for k, v in arrays.items()}
    nc = bacc.Bacc("TRN2", target_bir_lowering=False, num_devices=1)
    aps = {k: nc.dram_tensor(k, v.shape, mybir.dt.from_np(v.dtype), kind="ExternalInput").ap()
           for k, v in arrays.items()}
    out = nc.dram_tensor("out", (P, KT, S), F32, kind="ExternalOutput").ap()
    encoder_kernel(nc, out=out, **aps)
    r = run_bass_kernel_spmd(nc, [arrays], core_ids=[0])
    y = r.results[0]["out"]
    return np.ascontiguousarray(y.transpose(1, 0, 2).reshape(D, S).T[None])
```
